# Optimizing a Trainium2 kernel written in Bass

```python
import jax, jax.numpy as jnp
from jax import lax
import numpy as np

D_MODEL = 1024
BATCH = 1
SEQ = 256
DEPTH = 2

CHUNK = 64
N_MIXERS = 2
POOL_WINDOWS = (2, 4, 8, 16)
N_POOL_GROUPS = len(POOL_WINDOWS)
POOL_GROUP_DIM = D_MODEL // N_POOL_GROUPS
HEAD_DIM = 64
N_HEADS = D_MODEL // HEAD_DIM
Q_BLOCK = 128
D_FF_DENSE = ((8 * D_MODEL // 3 + 127) // 128) * 128
N_EXPERTS = 8
TOP_K = 2
D_FF_EXPERT = 7 * D_MODEL // 2
RMS_EPS = 1e-6
N_POOL_LAYERS = (DEPTH + 1) // 2
N_ATTN_LAYERS = DEPTH // 2
N_DENSE_LAYERS = (DEPTH + 1) // 2
N_MOE_LAYERS = DEPTH // 2
NEG_INF = -1e30

kernel_name = "hybrid_pool_fox_moe_trunk"

def rms_norm(x, g):
    xf = x.astype(jnp.float32)
    y = xf * lax.rsqrt(jnp.mean(xf * xf, axis=-1, keepdims=True) + RMS_EPS)
    return (y * g.astype(jnp.float32)).astype(x.dtype)

def pool_mixer(h, w_group, scale):
    B, S, D = h.shape
    hf = h.astype(jnp.float32)
    cum = jnp.cumsum(hf, axis=1)
    t = jnp.arange(S)
    outs = []
    for g, w in enumerate(POOL_WINDOWS):
        sl = slice(g * POOL_GROUP_DIM, (g + 1) * POOL_GROUP_DIM)
        c = cum[:, :, sl]
        c_lag = jnp.pad(c, ((0, 0), (w, 0), (0, 0)))[:, :S]
        count = jnp.minimum(t + 1, w).astype(jnp.float32)
        mean = (c - c_lag) / count[None, :, None]
        outs.append(mean - hf[:, :, sl])
    pooled = jnp.stack(outs, axis=2).astype(h.dtype)
    mixed = jnp.einsum('bsgc,gcd->bsgd', pooled, w_group).reshape(B, S, D)
    return mixed * scale

def forgetting_attention(h, w_in, b_f, w_out):
    B, S, D = h.shape
    proj = h @ w_in
    q, k, v, f_logit = jnp.split(proj, [D, 2 * D, 3 * D], axis=-1)
    q = q.reshape(B, S, N_HEADS, HEAD_DIM)
    k = k.reshape(B, S, N_HEADS, HEAD_DIM)
    v = v.reshape(B, S, N_HEADS, HEAD_DIM)
    log_f = jax.nn.log_sigmoid((f_logit + b_f).astype(jnp.float32))
    c = jnp.cumsum(log_f, axis=1).transpose(0, 2, 1)
    n_blk = S // Q_BLOCK
    q_blocks = q.reshape(B, n_blk, Q_BLOCK, N_HEADS, HEAD_DIM).transpose(1, 0, 3, 2, 4)
    c_blocks = c.reshape(B, N_HEADS, n_blk, Q_BLOCK).transpose(2, 0, 1, 3)
    pos_k = jnp.arange(S)
    scale = HEAD_DIM ** -0.5

    def one_block(args):
        q_i, c_i, i = args
        pos_q = i * Q_BLOCK + jnp.arange(Q_BLOCK)
        logits = jnp.einsum('bhqd,bshd->bhqs', q_i, k).astype(jnp.float32) * scale
        logits = logits + c_i[..., :, None] - c[:, :, None, :]
        mask = pos_q[:, None] >= pos_k[None, :]
        logits = jnp.where(mask[None, None], logits, NEG_INF)
        p = jax.nn.softmax(logits, axis=-1).astype(v.dtype)
        return jnp.einsum('bhqs,bshd->bqhd', p, v)

    o = lax.map(one_block, (q_blocks, c_blocks, jnp.arange(n_blk)))
    o = o.transpose(1, 0, 2, 3, 4).reshape(B, S, D)
    return o @ w_out

def swiglu(h, w_gate, w_up, w_down):
    return (jax.nn.silu(h @ w_gate) * (h @ w_up)) @ w_down

def moe_swiglu(h, w_router, w_gate, w_up, w_down):
    logits = (h @ w_router).astype(jnp.float32)
    top_val, top_idx = lax.top_k(logits, TOP_K)
    top_w = jax.nn.softmax(top_val, axis=-1)
    gates = jnp.sum(jax.nn.one_hot(top_idx, N_EXPERTS, dtype=jnp.float32) * top_w[..., None], axis=-2)
    gates = gates.astype(h.dtype)
    out = jnp.zeros_like(h)
    for e in range(N_EXPERTS):
        out = out + gates[..., e:e + 1] * swiglu(h, w_gate[e], w_up[e], w_down[e])
    return out

def setup_inputs(seed: int = 0) -> dict:
    key = jax.random.key(seed)
    ks = jax.random.split(key, 16)
    D, H = D_MODEL, N_HEADS

    def nrm(k, shape, fan_in):
        return jax.random.normal(k, shape, jnp.float32) * (fan_in ** -0.5)

    x = jax.random.normal(ks[0], (BATCH, SEQ, D), jnp.float32)
    norm_g = 1.0 + 0.05 * jax.random.normal(ks[1], (DEPTH, 4, D), jnp.float32)
    pool_w = nrm(ks[2], (N_POOL_LAYERS, N_POOL_GROUPS, POOL_GROUP_DIM, POOL_GROUP_DIM), POOL_GROUP_DIM)
    pool_scale = 1.0 + 0.1 * jax.random.normal(ks[3], (N_POOL_LAYERS, D), jnp.float32)
    attn_w_in = nrm(ks[4], (N_ATTN_LAYERS, D, 3 * D + H), D)
    attn_b_f = 3.0 + 0.5 * jax.random.normal(ks[5], (N_ATTN_LAYERS, H), jnp.float32)
    attn_w_out = nrm(ks[6], (N_ATTN_LAYERS, D, D), D)
    ffn_w_gate = nrm(ks[7], (N_DENSE_LAYERS, D, D_FF_DENSE), D)
    ffn_w_up = nrm(ks[8], (N_DENSE_LAYERS, D, D_FF_DENSE), D)
    ffn_w_down = nrm(ks[9], (N_DENSE_LAYERS, D_FF_DENSE, D), D_FF_DENSE)
    moe_w_router = nrm(ks[10], (N_MOE_LAYERS, D, N_EXPERTS), D)
    moe_w_gate = nrm(ks[11], (N_MOE_LAYERS, N_EXPERTS, D, D_FF_EXPERT), D)
    moe_w_up = nrm(ks[12], (N_MOE_LAYERS, N_EXPERTS, D, D_FF_EXPERT), D)
    moe_w_down = nrm(ks[13], (N_MOE_LAYERS, N_EXPERTS, D_FF_EXPERT, D), D_FF_EXPERT)
    return {"x": x, "norm_g": norm_g, "pool_w": pool_w, "pool_scale": pool_scale,
            "attn_w_in": attn_w_in, "attn_b_f": attn_b_f, "attn_w_out": attn_w_out,
            "ffn_w_gate": ffn_w_gate, "ffn_w_up": ffn_w_up, "ffn_w_down": ffn_w_down,
            "moe_w_router": moe_w_router, "moe_w_gate": moe_w_gate,
            "moe_w_up": moe_w_up, "moe_w_down": moe_w_down}

def reference(x, norm_g, pool_w, pool_scale, attn_w_in, attn_b_f, attn_w_out,
              ffn_w_gate, ffn_w_up, ffn_w_down,
              moe_w_router, moe_w_gate, moe_w_up, moe_w_down):
    for i in range(DEPTH):
        slot = i // 2
        h = rms_norm(x, norm_g[i, 0])
        if i % N_MIXERS == 0:
            y = pool_mixer(h, pool_w[slot], pool_scale[slot])
        else:
            y = forgetting_attention(h, attn_w_in[slot], attn_b_f[slot], attn_w_out[slot])
        x = x + rms_norm(y, norm_g[i, 1])
        h = rms_norm(x, norm_g[i, 2])
        if i % 2 == 0:
            y = swiglu(h, ffn_w_gate[slot], ffn_w_up[slot], ffn_w_down[slot])
        else:
            y = moe_swiglu(h, moe_w_router[slot], moe_w_gate[slot], moe_w_up[slot], moe_w_down[slot])
        x = x + rms_norm(y, norm_g[i, 3])
    return x


_drawn_inputs = setup_inputs


def setup_inputs(seed=0):
    import zlib

    import numpy as np

    out = dict(_drawn_inputs(seed))
    spreads = {}
    factors = {}
    for name, (base, spread) in spreads.items():
        noise = np.random.default_rng([zlib.crc32(name.encode()), seed]).standard_normal(out[name].shape)
        drawn = base * np.exp(spread * noise) if base else spread * noise
        out[name] = __import__('jax').numpy.asarray(drawn.astype(out[name].dtype))
    for name, factor in factors.items():
        out[name] = (out[name] * factor).astype(out[name].dtype)
    return out
```

```python
from contextlib import ExitStack

import numpy as np

import concourse.bass as bass
from concourse import mybir

P = 128
D = 1024
KB = D // P
T = 256
TB = T // P
HALF = 512
POOL_WINDOWS = (2, 4, 8, 16)
POOL_G = len(POOL_WINDOWS)
H = 16
HD = D // H
F_DENSE = 2816
FG = 256
N_FG = F_DENSE // FG
E = 8
F_EXP = 3584
N_EG = F_EXP // HALF
EPS = 1e-6
NEG_INF = -1e30

UNIT = 2048
RAW_SLOTS = 7
SPLIT_SLOTS = 3
FFN_U0 = 1
V_U0 = FFN_U0 + 3 * N_FG
QK_U0 = V_U0 + 4
OUT_U0 = QK_U0 + H // 2
MOE_U0 = OUT_U0 + 4
ROUND_UNITS = 6 * N_EG
X_ROUNDS = 3

C_IDENT = 0
C_TRI = 128
C_ONES = 256
C_TRIS = 384
C_MASK = 512
C_IOTA = 896
C_ALL = 1024

PRE_GAIN = (0, 2)


def trunk(nc, x_d, norm_g, pool_w, pool_scale, w_in, b_f, w_out, ffn_gate, ffn_up, ffn_down,
          w_router, moe_gate, moe_up, moe_down, consts_d, bands_d, heads_d, out_d):
    f32 = mybir.dt.float32
    f32r = mybir.dt.float32r
    i32 = mybir.dt.int32
    u32 = mybir.dt.uint32
    ALU = mybir.AluOpType
    ACT = mybir.ActivationFunctionType
    AX = mybir.AxisListType

    with ExitStack() as ctx:
        def sb(name, shape, dt=f32):
            return ctx.enter_context(nc.sbuf_tensor(name, shape, dt))

        def sem(name):
            return ctx.enter_context(nc.semaphore(name))

        raw = sb("raw", [P, RAW_SLOTS, UNIT])
        w_hi = sb("w_hi", [P, SPLIT_SLOTS, UNIT], f32r)
        w_lo = sb("w_lo", [P, SPLIT_SLOTS, UNIT], f32r)
        x = sb("x", [P, TB, D])
        xn = sb("xn", [P, TB, D])
        h_hi = sb("h_hi", [P, KB, T], f32r)
        h_lo = sb("h_lo", [P, KB, T], f32r)
        with nc.sbuf_tensor("o_hi", [P, KB, T], f32r) as o_hi:
            pass
        y = sb("y", [P, TB, D])
        gain = sb("gain", [P, 2, D])
        consts = sb("consts", [P, C_ALL])
        g_rows = sb("g_rows", [64, P])
        g_col = sb("g_col", [P, 64])
        sums = sb("sums", [P, 8, TB, 2])
        mean = sb("mean", [P, 8, TB])
        newton = sb("newton", [P, TB])
        rstd = sb("rstd", [P, 8, TB])
        silu = sb("silu", [P, HALF])
        act = sb("act", [P, HALF])
        aT_hi = sb("aT_hi", [P, HALF], f32r)
        aT_lo = sb("aT_lo", [P, HALF], f32r)
        small_w = sb("small_w", [P, KB, H + E])
        wf2 = sb("wf2", [P, KB, 2 * H], f32r)
        wr2 = sb("wr2", [P, KB, 2 * E], f32r)
        bf = sb("bf", [P, H])
        with nc.sbuf_tensor("bands", [P, POOL_G, 3 * P], f32) as bands:
            pass
        with ExitStack() as attn:
            def sa(name, shape, dt=f32):
                return attn.enter_context(nc.sbuf_tensor(name, shape, dt))
            head_row = sa("head_row", [H, H, P])
            v = sa("v", [P, TB, D])
            qk = sa("qk", [P, 2 * T])
            logit = sa("logit", [P, 2, 3 * P])
            pT = sa("pT", [P, 2, 3 * P])
            o_lo = sa("o_lo", [P, KB, T], f32r)
            fz = sa("fz", [P, TB, H])
            fe = sa("fe", [P, TB, H])
            fl = sa("fl", [P, TB, H])
            logf = sa("logf", [P, TB, H])
            ncT = sa("ncT", [H, T])
            mx = sa("mx", [P, H // 2, 4])
            nmx = sa("nmx", [P, H // 2, 4])
            den = sa("den", [P, H // 2, 4])
            rden = sa("rden", [P, H // 2, 4])
        ye = sb("ye", [P, D])
        sel = sb("sel", [P, TB, P])
        gsel = sb("gsel", [P, TB, P])
        gselT = sb("gselT", [P, T])
        sel2 = sb("sel2", [P, TB, P])
        lg = sb("lg", [P, TB, E])
        top = sb("top", [P, TB, 8])
        topi = sb("topi", [P, TB, 8], u32)
        topf = sb("topf", [P, TB, 2])
        gate = sb("gate", [P, TB, 2])
        gtmp = sb("gtmp", [P, TB, 3])
        m12 = sb("m12", [P, TB, 2, E])
        mboth = sb("mboth", [P, TB, E])
        rank = sb("rank", [P, TB, E])
        over = sb("over", [P, TB, E])
        prod = sb("prod", [P, TB, 2, E])
        gpos = sb("gpos", [P, TB, 2])
        ctab = sb("ctab", [P, 8, E])
        rtab = sb("rtab", [1, 4])
        rtab_i = sb("rtab_i", [1, 4], i32)
        bank = [ctx.enter_context(nc.psum_tensor(f"bank{i}", [P, HALF], f32)) for i in range(8)]

        ident = consts[:, C_IDENT:C_IDENT + P]

        raw_in = [sem(f"raw_in{i}") for i in range(RAW_SLOTS)]
        hi_ready = sem("hi_ready")
        lo_ready = sem("lo_ready")
        unit_used = sem("unit_used")
        x_in = sem("x_in")
        consts_in = sem("consts_in")
        bands_in = sem("bands_in")
        grows_in = sem("grows_in")
        heads_in = sem("heads_in")
        small_in = sem("small_in")
        gain_in = [sem("gain_in0"), sem("gain_in1")]
        out_in = sem("out_in")
        gcol_psum = sem("gcol_psum")
        gcol_done = sem("gcol_done")
        sq_done = sem("sq_done")
        dve = sem("dve")
        xn_done = sem("xn_done")
        tr_done = sem("tr_done")
        h_hi_done = sem("h_hi_done")
        h_lo_done = sem("h_lo_done")
        y_done = sem("y_done")
        x_done = sem("x_done")
        silu_done = sem("silu_done")
        act_done = sem("act_done")
        aT_psum = sem("aT_psum")
        aT_hi_done = sem("aT_hi_done")
        aT_lo_done = sem("aT_lo_done")
        small_hi = sem("small_hi")
        small_lo = sem("small_lo")
        f_psum = sem("f_psum")
        fz_done = sem("fz_done")
        fe_done = sem("fe_done")
        fl_done = sem("fl_done")
        logf_done = sem("logf_done")
        c_psum = sem("c_psum")
        ncT_done = sem("ncT_done")
        v_done = sem("v_done")
        q_done = sem("q_done")
        k_done = sem("k_done")
        s_psum = sem("s_psum")
        mx_done = sem("mx_done")
        exp_done = sem("exp_done")
        p_done = sem("p_done")
        pT_psum = sem("pT_psum")
        pT_done = sem("pT_done")
        o_psum = sem("o_psum")
        o_hi_done = sem("o_hi_done")
        o_lo_done = sem("o_lo_done")
        lg_psum = sem("lg_psum")
        gap_done = sem("gap_done")
        gexp_done = sem("gexp_done")
        m_done = sem("m_done")
        rank_psum = sem("rank_psum")
        rtab_done = sem("rtab_done")
        sel_done = sem("sel_done")
        gT_psum = sem("gT_psum")
        gT_done = sem("gT_done")
        he_psum = sem("he_psum")
        he_hi_done = sem("he_hi_done")
        he_lo_done = sem("he_lo_done")
        ye_act = sem("ye_act")
        ye_dve = sem("ye_dve")
        sc_psum = sem("sc_psum")
        acc_done = sem("acc_done")
        selc = sem("selc")

        landed, on_slot = [], [0] * RAW_SLOTS
        for u in range(MOE_U0):
            on_slot[u % RAW_SLOTS] += 32 if QK_U0 <= u < OUT_U0 else 16
            landed.append(on_slot[u % RAW_SLOTS])

        def moe_landed(r, j):
            s = (MOE_U0 + j) % RAW_SLOTS
            return r * (16 * ROUND_UNITS // RAW_SLOTS) + (on_slot[s] + 16 * (j // RAW_SLOTS + 1))

        def u_gate(g):
            return FFN_U0 + (0 if g == 0 else 3 * g - 1 + 0)

        def u_up(g):
            return u_gate(g) + 1

        def u_down(g):
            return FFN_U0 + (3 * g + 4 if g < N_FG - 1 else 3 * g + 2)

        def j_gate(g):
            return 0 if g == 0 else 6 * g - 2

        def j_up(g):
            return j_gate(g) + 2

        def j_down(g):
            return 6 * g + 8 if g < N_EG - 1 else 6 * g + 4

        def part(t, s, n):
            return t[:, s, :].rearrange("p (b n) -> p b n", n=n)

        block = ctx.enter_context(nc.Block())

        @block.sync
        def _(sp):
            def rows(w, first, blocks, col, n):
                return w[first * P:(first + blocks) * P, col:col + n].rearrange("(b p) n -> p b n", p=P)

            def load(u, src, n):
                if u >= RAW_SLOTS:
                    sp.wait_ge(lo_ready, u - RAW_SLOTS + 1)
                sp.dma_start(part(raw, u % RAW_SLOTS, n), src).then_inc(raw_in[u % RAW_SLOTS], 16)

            for tb in range(TB):
                sp.dma_start(x[:, tb, :], x_d[0, tb * P:(tb + 1) * P, :]).then_inc(x_in, 16)
            load(0, pool_w[0].rearrange("g (b p) n -> p (g b) n", p=P), FG)
            for u in range(FFN_U0, V_U0):
                for g in range(N_FG):
                    if u == u_gate(g):
                        load(u, rows(ffn_gate[0], 0, KB, g * FG, FG), FG)
                    elif u == u_up(g):
                        load(u, rows(ffn_up[0], 0, KB, g * FG, FG), FG)
                    elif u == u_down(g):
                        load(u, rows(ffn_down[0], 2 * g, 2, 0, D), D)
                if u == FFN_U0 + 6:
                    sp.wait_ge(x_done, 2)
                    sp.dma_start(gain[:, 0, :], norm_g[0, 3:4, :].to_broadcast([P, D])).then_inc(gain_in[0], 16)
                    sp.dma_start(gain[:, 1, :], norm_g[1, 1:2, :].to_broadcast([P, D])).then_inc(gain_in[1], 16)
            for i in range(4):
                load(V_U0 + i, rows(w_in[0], 4 * (i % 2), 4, 2 * D + (i // 2) * HALF, HALF), HALF)
            for j in range(H // 2):
                u = QK_U0 + j
                sp.wait_ge(lo_ready, u - RAW_SLOTS + 1)
                for i in range(2):
                    sp.dma_start(part(raw, u % RAW_SLOTS, T)[:, :, i * P:(i + 1) * P],
                                 rows(w_in[0], 0, KB, i * D + j * P, P)).then_inc(raw_in[u % RAW_SLOTS], 16)
            for i in range(4):
                load(OUT_U0 + i, rows(w_out[0], 2 * i, 2, 0, D), D)

            def expert(r, e):
                gate_e = moe_gate[0, bass.ds(e, 1), :, :].rearrange("a k n -> (a k) n")
                up_e = moe_up[0, bass.ds(e, 1), :, :].rearrange("a k n -> (a k) n")
                down_e = moe_down[0, bass.ds(e, 1), :, :].rearrange("a k n -> (a k) n")

                def load_e(j, src, n):
                    s = (MOE_U0 + j) % RAW_SLOTS
                    sp.wait_ge(lo_ready, r * ROUND_UNITS + (MOE_U0 + j - RAW_SLOTS + 1))
                    sp.dma_start(part(raw, s, n), src).then_inc(raw_in[s], 16)

                for g in range(-1, N_EG):
                    for i in range(2):
                        if g < N_EG - 1:
                            load_e(j_gate(g + 1) + i, rows(gate_e, 4 * i, 4, (g + 1) * HALF, HALF), HALF)
                    for i in range(2):
                        if g < N_EG - 1:
                            load_e(j_up(g + 1) + i, rows(up_e, 4 * i, 4, (g + 1) * HALF, HALF), HALF)
                    for i in range(2):
                        if g >= 0:
                            load_e(j_down(g) + i, rows(down_e, 4 * g + 2 * i, 2, 0, D), D)

            with sp.Fori(0, E) as r:
                expert(r, r)
            sp.wait_ge(x_done, 4)
            sp.dma_start(gain[:, 0, :], norm_g[1, 3:4, :].to_broadcast([P, D])).then_inc(gain_in[0], 16)
            sp.wait_ge(rtab_done, 1)
            rounds = sp.value_load(rtab_i[0:1, 0:1], min_val=E, max_val=E + X_ROUNDS)
            for i in range(X_ROUNDS):
                e_x = sp.value_load(rtab_i[0:1, 1 + i:2 + i], min_val=0, max_val=E - 1)
                with sp.If(rounds > E + i):
                    expert(E + i, e_x)
            for tb in range(TB):
                sp.wait_ge(x_done, 2 * 3 + tb + 1)
                sp.dma_start(out_d[0, tb * P:(tb + 1) * P, :], x[:, tb, :]).then_inc(out_in, 16)
            sp.wait_ge(out_in, 16 * TB)

        @block.scalar
        def _(sc):
            sc.dma_start(consts[:, :], consts_d).then_inc(consts_in, 16)
            sc.dma_start(g_rows[:, :], norm_g.rearrange("l j (k p) -> (l j k) p", p=P)).then_inc(grows_in, 16)
            sc.dma_start(bands[:, :, :], bands_d).then_inc(bands_in, 16)
            sc.dma_start(gain[:, 0, :], pool_scale.to_broadcast([P, D])).then_inc(gain_in[0], 16)
            sc.dma_start(gain[:, 1, :], norm_g[0, 1:2, :].to_broadcast([P, D])).then_inc(gain_in[1], 16)
            sc.dma_start(small_w[:, :, 0:H],
                         w_in[0, :, 3 * D:3 * D + H].rearrange("(k p) n -> p k n", p=P)).then_inc(small_in, 16)
            sc.dma_start(small_w[:, :, H:H + E],
                         w_router[0].rearrange("(k p) n -> p k n", p=P)).then_inc(small_in, 16)
            sc.dma_start(bf[:, :], b_f.to_broadcast([P, H])).then_inc(small_in, 16)

            def split_hi(slot, raw_slot, arrived, used):
                sc.wait_ge(raw_in[raw_slot], arrived)
                if used is not None:
                    sc.wait_ge(unit_used, used)
                nc.scalar.activation(w_hi[:, slot, :], raw[:, raw_slot, :], ACT.Copy).then_inc(hi_ready, 1)

            def hi(u):
                split_hi(u % SPLIT_SLOTS, u % RAW_SLOTS, landed[u],
                         u - SPLIT_SLOTS + 1 if u >= SPLIT_SLOTS else None)

            def squares(n, tb):
                nc.scalar.activation(xn[:, tb, :], x[:, tb, :], ACT.Square,
                                     accum_out=sums[:, n, tb, 0:1]).then_inc(sq_done, 1)

            def post_squares(n, source):
                for tb in range(TB):
                    for half in range(2):
                        nc.scalar.activation(xn[:, tb, half * HALF:(half + 1) * HALF], source(tb, half),
                                             ACT.Square, accum_out=sums[:, n, tb, half:half + 1]).then_inc(sq_done, 1)

            def input_hi(phase):
                for k in range(KB):
                    if k % 2 == 0:
                        sc.wait_ge(tr_done, 4 * phase + k // 2 + 1)
                    col = (phase // 2) * 32 + PRE_GAIN[phase % 2] * 8 + k
                    nc.scalar.activation(h_hi[:, k, :], bank[k // 2][:, (k % 2) * T:(k % 2 + 1) * T], ACT.Copy,
                                         scale=g_col[:, col:col + 1]).then_inc(h_hi_done, 1)

            for tb in range(TB):
                sc.wait_ge(x_in, 32)
                squares(0, tb)
            hi(0)
            sc.wait_ge(gcol_done, 1)
            input_hi(0)
            hi(1)
            hi(2)
            sc.wait_ge(y_done, 4)
            post_squares(1, lambda tb, half: y[:, tb, half * HALF:(half + 1) * HALF])
            for tb in range(TB):
                sc.wait_ge(x_done, tb + 1)
                squares(2, tb)
            input_hi(1)
            sc.wait_ge(small_in, 48)
            nc.scalar.activation(wf2[:, :, 0:H], small_w[:, :, 0:H], ACT.Copy).then_inc(small_hi, 1)
            nc.scalar.activation(wr2[:, :, 0:E], small_w[:, :, H:H + E], ACT.Copy).then_inc(small_hi, 1)

            def silu_group(q, used):
                sc.wait_ge(unit_used, used)
                if q is not None:
                    sc.wait_ge(act_done, q)
                nc.scalar.activation(silu[:, :], bank[0][:, :], ACT.Silu).then_inc(silu_done, 1)

            def aT_high(q):
                sc.wait_ge(aT_psum, q)
                nc.scalar.activation(aT_hi[:, :], bank[2][:, :],
                                     ACT.Copy).then_inc(aT_hi_done, 1)

            hi(3)
            silu_group(None, u_gate(0) + 1)
            for g in range(N_FG):
                if g < N_FG - 1:
                    hi(u_up(g + 1))
                    hi(u_down(g))
                    silu_group(g + 1, u_gate(g + 1) + 1)
                    if g > 0:
                        sc.wait_ge(unit_used, u_down(g - 1) + 1)
                    aT_high(g + 1)
                    hi(u_down(g) + 1)
                else:
                    hi(V_U0)
                    sc.wait_ge(unit_used, u_down(g - 1) + 1)
                    aT_high(g + 1)
                    hi(V_U0 + 1)
            sc.wait_ge(unit_used, V_U0)
            post_squares(3, lambda tb, half: bank[4 + 2 * tb + half][:, :])
            for tb in range(TB):
                sc.wait_ge(x_done, 2 + tb + 1)
                squares(4, tb)
            input_hi(2)
            hi(V_U0 + 2)
            sc.wait_ge(fz_done, 1)
            nc.scalar.activation(fe[:, :, :], fe[:, :, :], ACT.Exp, scale=-1.0).then_inc(fe_done, 1)
            sc.wait_ge(fe_done, 1)
            nc.scalar.activation(fl[:, :, :], fe[:, :, :], ACT.Ln, bias=1.0).then_inc(fl_done, 1)
            sc.wait_ge(c_psum, 1)
            nc.scalar.activation(ncT[:, :], bank[3][0:H, 0:T], ACT.Copy, scale=-1.0).then_inc(ncT_done, 1)
            hi(V_U0 + 3)
            hi(QK_U0)
            for half in range(2):
                sc.wait_ge(unit_used, V_U0 + 2 * half + 2)
                for tb in range(TB):
                    nc.scalar.activation(v[:, tb, half * HALF:(half + 1) * HALF], bank[4 + 2 * half + tb][:, :],
                                         ACT.Copy).then_inc(v_done, 1)
                if half == 0:
                    hi(QK_U0 + 1)

            def pT_copy(j):
                for i in range(2):
                    sc.wait_ge(pT_psum, 2 * j + i + 1)
                    if j > 0:
                        sc.wait_ge(o_psum, j)
                    nc.scalar.activation(pT[:, i, :], bank[4 + i][:, 0:3 * P], ACT.Copy).then_inc(pT_done, 1)

            def out_hi(j):
                sc.wait_ge(o_psum, j + 1)
                nc.scalar.activation(o_hi[:, j, :], bank[6][:, 0:T], ACT.Copy).then_inc(o_hi_done, 1)

            for j in range(H // 2):
                hi(QK_U0 + j + 2)
                sc.wait_ge(unit_used, QK_U0 + j + 1)
                if j > 0:
                    sc.wait_ge(s_psum, 2 * j)
                nc.scalar.activation(qk[:, 0:T], bank[0][:, 0:T], ACT.Copy, scale=HD ** -0.5).then_inc(q_done, 1)
                if j > 0:
                    pT_copy(j - 1)
                    out_hi(j - 1)
                for i in range(2):
                    for b in range(TB):
                        sc.wait_ge(mx_done, 2 * j + i + 1)
                        nc.scalar.activation(logit[:, i, b * P:(2 * b + 1) * P], logit[:, i, b * P:(2 * b + 1) * P],
                                             ACT.Exp, bias=nmx[:, j, 2 * i + b:2 * i + b + 1],
                                             accum_out=den[:, j, 2 * i + b:2 * i + b + 1]).then_inc(exp_done, 1)
            pT_copy(H // 2 - 1)
            out_hi(H // 2 - 1)
            for i in range(2):
                hi(OUT_U0 + 2 + i)
            sc.wait_ge(unit_used, MOE_U0)
            post_squares(5, lambda tb, half: bank[(1, 2, 3, 7)[2 * tb + half]][:, :])
            for tb in range(TB):
                sc.wait_ge(x_done, 4 + tb + 1)
                squares(6, tb)
            input_hi(3)
            sc.wait_ge(gap_done, 1)
            nc.scalar.activation(gtmp[:, :, 1:2], gtmp[:, :, 0:1], ACT.Exp).then_inc(gexp_done, 1)

            def he_hi(r1):
                for k in range(KB):
                    if k == 0:
                        sc.wait_ge(he_psum, r1)
                    nc.scalar.activation(h_hi[:, k, 0:P], bank[6 + k // 4][:, (k % 4) * P:(k % 4 + 1) * P], ACT.Copy,
                                         scale=g_col[:, 48 + k:49 + k]).then_inc(he_hi_done, 1)

            he_hi(1)
            sc.wait_ge(rtab_done, 1)
            rounds = sc.value_load(rtab_i[0:1, 0:1], min_val=E, max_val=E + X_ROUNDS)
            with sc.Fori(0, rounds) as r:
                def hi_e(j):
                    split_hi((MOE_U0 + j) % SPLIT_SLOTS, (MOE_U0 + j) % RAW_SLOTS, moe_landed(r, j),
                             r * ROUND_UNITS + (MOE_U0 + j - SPLIT_SLOTS + 1))

                def used(j):
                    return r * ROUND_UNITS + (MOE_U0 + j + 1)

                q0 = r * N_EG + N_FG
                for j in range(4):
                    hi_e(j)
                silu_group(q0, used(j_gate(0) + 1))
                sc.wait_ge(gT_psum, r + 1)
                nc.scalar.activation(gselT[:, :], bank[3][:, 0:T], ACT.Copy).then_inc(gT_done, 1)
                for g in range(N_EG):
                    if g < N_EG - 1:
                        for j in range(j_gate(g + 1), j_gate(g + 1) + 4):
                            hi_e(j)
                        silu_group(q0 + (g + 1), used(j_gate(g + 1) + 1))
                        if g > 0:
                            sc.wait_ge(unit_used, used(j_down(g - 1) + 1))
                        aT_high(q0 + (g + 1))
                        hi_e(j_down(g))
                        hi_e(j_down(g) + 1)
                    else:
                        hi_e(j_down(g))
                        hi_e(j_down(g) + 1)
                        sc.wait_ge(unit_used, used(j_down(g - 1) + 1))
                        aT_high(q0 + (g + 1))
                he_hi(r + 2)
                sc.wait_ge(unit_used, used(ROUND_UNITS - 1))
                sc.wait_ge(sc_psum, r)
                nc.scalar.activation(ye[:, 0:HALF], bank[4][:, :], ACT.Copy).then_inc(ye_act, 1)
            sc.wait_ge(acc_done, rounds * 4 + 1)
            post_squares(7, lambda tb, half: y[:, tb, half * HALF:(half + 1) * HALF])

        @block.vector
        def _(ve):
            steps = [0]

            def link(ins):
                steps[0] += 1
                ins.then_inc(dve, 1)
                ve.wait_ge(dve, steps[0])

            def split_lo(slot, raw_slot, ready):
                ve.wait_ge(hi_ready, ready)
                nc.vector.tensor_tensor(w_lo[:, slot, :], raw[:, raw_slot, :], w_hi[:, slot, :].bitcast(f32),
                                        ALU.subtract).then_inc(lo_ready, 1)

            def lo(u):
                split_lo(u % SPLIT_SLOTS, u % RAW_SLOTS, u + 1)

            def roots(n, before):
                m, r, t = mean[:, n, :], rstd[:, n, :], newton[:, :]
                ve.wait_ge(sq_done, before + (4 if n % 2 else 2))
                if n % 2:
                    link(nc.vector.tensor_tensor(m, sums[:, n, :, 0], sums[:, n, :, 1], ALU.add))
                    link(nc.vector.tensor_scalar(m, m, 1.0 / D, EPS, ALU.mult, ALU.add))
                else:
                    link(nc.vector.tensor_scalar(m, sums[:, n, :, 0], 1.0 / D, EPS, ALU.mult, ALU.add))
                link(nc.vector.tensor_scalar(r.bitcast(i32), m.bitcast(i32), -0.5, float(0x5F3759DF),
                                             ALU.mult, ALU.add))
                for _ in range(3):
                    link(nc.vector.tensor_tensor(t, r, r, ALU.mult))
                    link(nc.vector.tensor_tensor(t, t, m, ALU.mult))
                    link(nc.vector.tensor_scalar(t, t, -0.5, 1.5, ALU.mult, ALU.add))
                    link(nc.vector.tensor_tensor(r, r, t, ALU.mult))

            def norm_x(n):
                roots(n, 3 * n)
                for tb in range(TB):
                    nc.vector.tensor_scalar(xn[:, tb, :], x[:, tb, :], rstd[:, n, tb:tb + 1], None,
                                            ALU.mult).then_inc(xn_done, 1)

            def add_normed(n, source, slot, arrived):
                ve.wait_ge(gain_in[slot], arrived)
                roots(n, 3 * n - 1)
                for tb in range(TB):
                    for half in range(2):
                        cols = slice(half * HALF, (half + 1) * HALF)
                        step = nc.vector.scalar_tensor_tensor(y[:, tb, cols], source(tb, half), rstd[:, n, tb:tb + 1],
                                                              gain[:, slot, cols], ALU.mult, ALU.mult)
                    link(step)
                    nc.vector.tensor_tensor(x[:, tb, :], x[:, tb, :], y[:, tb, :], ALU.add).then_inc(x_done, 1)

            def input_lo(phase):
                for k in range(KB):
                    if k % 2 == 0:
                        ve.wait_ge(h_hi_done, KB * phase + k + 2)
                    col = (phase // 2) * 32 + PRE_GAIN[phase % 2] * 8 + k
                    nc.vector.scalar_tensor_tensor(h_lo[:, k, :], bank[k // 2][:, (k % 2) * T:(k % 2 + 1) * T],
                                                   g_col[:, col:col + 1], h_hi[:, k, :].bitcast(f32),
                                                   ALU.mult, ALU.subtract).then_inc(h_lo_done, 1)

            ve.wait_ge(gcol_psum, 1)
            nc.vector.tensor_copy(g_col[:, :], bank[7][:, 0:64]).then_inc(gcol_done, 1)
            ve.wait_ge(x_in, 32)
            norm_x(0)
            lo(0)
            ve.wait_ge(gcol_done, 1)
            input_lo(0)
            lo(1)
            lo(2)
            ve.wait_ge(gain_in[0], 16)
            ve.wait_ge(unit_used, 1)
            for tb in range(TB):
                for half in range(2):
                    cols = slice(half * HALF, (half + 1) * HALF)
                    nc.vector.tensor_tensor(y[:, tb, cols], bank[4 + 2 * tb + half][:, :], gain[:, 0, cols],
                                            ALU.mult).then_inc(y_done, 1)
            ve.wait_ge(y_done, 4)
            add_normed(1, lambda tb, half: y[:, tb, half * HALF:(half + 1) * HALF], 1, 16)
            norm_x(2)
            input_lo(1)
            for i, (wide, at, n) in enumerate(((wf2, 0, H), (wr2, H, E))):
                ve.wait_ge(small_hi, i + 1)
                nc.vector.tensor_tensor(wide[:, :, n:2 * n], small_w[:, :, at:at + n], wide[:, :, 0:n].bitcast(f32),
                                        ALU.subtract).then_inc(small_lo, 1)

            def gated(q, used):
                ve.wait_ge(silu_done, q)
                ve.wait_ge(unit_used, used)
                ve.wait_ge(aT_psum, q - 1) if not isinstance(q, int) or q > 1 else None
                nc.vector.tensor_tensor(act[:, :], silu[:, :], bank[1][:, :], ALU.mult).then_inc(act_done, 1)

            def aT_low(q):
                ve.wait_ge(aT_hi_done, q)
                nc.vector.tensor_tensor(aT_lo[:, :], bank[2][:, :], aT_hi[:, :].bitcast(f32),
                                        ALU.subtract).then_inc(aT_lo_done, 1)

            lo(3)
            gated(1, u_up(0) + 1)
            for g in range(N_FG):
                if g < N_FG - 1:
                    lo(u_up(g + 1))
                    lo(u_down(g))
                    aT_low(g + 1)
                    lo(u_down(g) + 1)
                    gated(g + 2, u_up(g + 1) + 1)
                else:
                    lo(V_U0)
                    aT_low(g + 1)
                    lo(V_U0 + 1)
            add_normed(3, lambda tb, half: bank[4 + 2 * tb + half][:, :], 0, 32)
            norm_x(4)
            input_lo(2)
            ve.wait_ge(small_in, 48)
            ve.wait_ge(f_psum, 1)
            for tb in range(TB):
                link(nc.vector.tensor_tensor(fz[:, tb, :], bank[6][:, tb * 2 * H:tb * 2 * H + H], bf[:, :], ALU.add))
                link(nc.vector.tensor_tensor(fz[:, tb, :], bank[6][:, tb * 2 * H + H:(tb + 1) * 2 * H],
                                             fz[:, tb, :], ALU.add))
            nc.vector.scalar_tensor_tensor(fe[:, :, :], fz[:, :, :], -1.0, fz[:, :, :], ALU.mult, ALU.max).then_inc(fz_done, 1)
            lo(V_U0 + 2)
            ve.wait_ge(fl_done, 1)
            nc.vector.scalar_tensor_tensor(logf[:, :, :], fz[:, :, :], 0.0, fl[:, :, :], ALU.min,
                                           ALU.subtract).then_inc(logf_done, 1)
            lo(V_U0 + 3)
            lo(QK_U0)
            lo(QK_U0 + 1)

            def out_lo(j):
                ve.wait_ge(o_hi_done, j + 1)
                nc.vector.tensor_tensor(o_lo[:, j, :], bank[6][:, 0:T], o_hi[:, j, :].bitcast(f32),
                                        ALU.subtract).then_inc(o_lo_done, 1)

            for j in range(H // 2):
                lo(QK_U0 + j + 2)
                ve.wait_ge(q_done, j + 1)
                if j > 0:
                    ve.wait_ge(s_psum, 2 * j)
                nc.vector.tensor_copy(qk[:, T:2 * T], bank[0][:, T:2 * T]).then_inc(k_done, 1)
                if j > 0:
                    out_lo(j - 1)
                for i in range(2):
                    ve.wait_ge(s_psum, 2 * j + i + 1)
                    if j > 0:
                        ve.wait_ge(pT_psum, 2 * (j - 1) + i + 1)
                    for b in range(TB):
                        step = nc.vector.tensor_tensor_reduce(
                            out=logit[:, i, b * P:(2 * b + 1) * P], in0=bank[1 + i][:, b * P:(2 * b + 1) * P],
                            in1=consts[:, C_MASK + b * P:C_MASK + (2 * b + 1) * P], scale=1.0, scalar=NEG_INF,
                            op0=ALU.add, op1=ALU.max, accum_out=mx[:, j, 2 * i + b:2 * i + b + 1])
                    link(step)
                    nc.vector.tensor_scalar(nmx[:, j, 2 * i:2 * i + 2], mx[:, j, 2 * i:2 * i + 2], -1.0, None,
                                            ALU.mult).then_inc(mx_done, 1)
                for i in range(2):
                    ve.wait_ge(exp_done, 4 * j + 2 * i + 2)
                    link(nc.vector.reciprocal(rden[:, j, 2 * i:2 * i + 2], den[:, j, 2 * i:2 * i + 2]))
                    for b in range(TB):
                        lt = logit[:, i, b * P:(2 * b + 1) * P]
                        step = nc.vector.tensor_scalar(lt, lt, rden[:, j, 2 * i + b:2 * i + b + 1], None, ALU.mult)
                    step.then_inc(p_done, 1)
            out_lo(H // 2 - 1)
            for i in range(2):
                lo(OUT_U0 + 2 + i)
            add_normed(5, lambda tb, half: bank[(1, 2, 3, 7)[2 * tb + half]][:, :], 1, 32)
            norm_x(6)
            input_lo(3)
            iota = consts[:, C_IOTA:C_IOTA + P]
            iota8 = consts[:, C_IOTA:C_IOTA + E]
            count, big, more, incl, shift, base = (ctab[:, i, :] for i in range(6))
            link(nc.vector.tensor_scalar(base, iota8, float(P), None, ALU.mult))
            ve.wait_ge(lg_psum, 1)
            for tb in range(TB):
                link(nc.vector.tensor_copy(lg[:, tb, :], bank[4][:, tb * 2 * E:tb * 2 * E + E]))
                link(nc.vector.tensor_tensor(lg[:, tb, :], bank[4][:, tb * 2 * E + E:(tb + 1) * 2 * E], lg[:, tb, :],
                                             ALU.add))
                link(nc.vector.max(top[:, tb, :], lg[:, tb, :]))
                link(nc.vector.max_index(topi[:, tb, :], top[:, tb, :], lg[:, tb, :]))
            link(nc.vector.tensor_copy(topf[:, :, :], topi[:, :, 0:2]))
            nc.vector.tensor_tensor(gtmp[:, :, 0:1], top[:, :, 1:2], top[:, :, 0:1], ALU.subtract).then_inc(gap_done, 1)
            for tb in range(TB):
                for i in range(2):
                    step = nc.vector.tensor_scalar(m12[:, tb, i, :], iota8, topf[:, tb, i:i + 1], None, ALU.is_equal)
            link(step)
            nc.vector.tensor_tensor(mboth[:, :, :], m12[:, :, 0, :], m12[:, :, 1, :], ALU.add).then_inc(m_done, 1)
            ve.wait_ge(gexp_done, 1)
            link(nc.vector.tensor_scalar(gtmp[:, :, 2:3], gtmp[:, :, 1:2], 1.0, None, ALU.add))
            link(nc.vector.reciprocal(gate[:, :, 0:1], gtmp[:, :, 2:3]))
            link(nc.vector.tensor_tensor(gate[:, :, 1:2], gate[:, :, 0:1], gtmp[:, :, 1:2], ALU.mult))
            ve.wait_ge(rank_psum, 1)
            link(nc.vector.tensor_copy(rank[:, :, :], bank[5][:, 0:TB * E].rearrange("p (b e) -> p b e", e=E)))
            link(nc.vector.tensor_copy(count, bank[5][:, TB * E:(TB + 1) * E]))
            link(nc.vector.tensor_scalar(big, count, float(P), None, ALU.is_gt))
            link(nc.vector.tensor_tensor_scan(incl, big, big, 0.0, ALU.add, ALU.bypass))
            link(nc.vector.tensor_tensor(more, incl, big, ALU.subtract))
            link(nc.vector.tensor_scalar(shift, more, float(P), float(P * (E - 1)), ALU.mult, ALU.add))
            link(nc.vector.tensor_tensor(shift, shift, base, ALU.subtract))
            link(nc.vector.tensor_scalar(over[:, :, :], rank[:, :, :], float(P), None, ALU.is_ge))
            for tb in range(TB):
                link(nc.vector.tensor_tensor(over[:, tb, :], over[:, tb, :], shift, ALU.mult))
                link(nc.vector.tensor_tensor(rank[:, tb, :], rank[:, tb, :], base, ALU.add))
            link(nc.vector.tensor_tensor(rank[:, :, :], rank[:, :, :], over[:, :, :], ALU.add))
            for i in range(2):
                link(nc.vector.tensor_tensor(prod[:, :, i, :], m12[:, :, i, :], rank[:, :, :], ALU.mult))
            link(nc.vector.reduce_sum(gpos[:, :, :], prod[:, :, :, :], AX.X))
            link(nc.vector.tensor_scalar(rtab[:, 0:1], ctab[0:1, 3, E - 1:E], float(E), None, ALU.add))
            for i in range(X_ROUNDS):
                link(nc.vector.tensor_scalar(ctab[0:1, 6, :], ctab[0:1, 3, :], float(i), None, ALU.is_le))
                link(nc.vector.reduce_sum(rtab[:, 1 + i:2 + i], ctab[0:1, 6, :], AX.X))
            link(nc.vector.tensor_scalar(rtab[:, 1:4], rtab[:, 1:4], float(E - 1), None, ALU.min))
            nc.vector.tensor_copy(rtab_i[:, :], rtab[:, :]).then_inc(rtab_done, 1)

            def select(before):
                n = [0]

                def then(ins):
                    n[0] += 1
                    ins.then_inc(selc, 1)
                    return before + n[0]

                for tb in range(TB):
                    for i, (to, to_gated) in enumerate(((sel, gsel), (sel2, None))):
                        at = then(nc.vector.tensor_scalar(to[:, tb, :], iota, gpos[:, tb, i:i + 1], None, ALU.is_equal))
                ve.wait_ge(selc, at)
                for tb in range(TB):
                    at = then(nc.vector.tensor_scalar(gsel[:, tb, :], sel[:, tb, :], gate[:, tb, 0:1], None, ALU.mult))
                ve.wait_ge(selc, at)
                for tb in range(TB):
                    at = then(nc.vector.scalar_tensor_tensor(gsel[:, tb, :], sel2[:, tb, :], gate[:, tb, 1:2],
                                                             gsel[:, tb, :], ALU.mult, ALU.add))
                nc.vector.tensor_tensor(sel[:, :, :], sel[:, :, :], sel2[:, :, :], ALU.add)
                nc.vector.tensor_scalar(gpos[:, :, :], gpos[:, :, :], float(-P), None, ALU.add).then_inc(sel_done, 1)
                return n[0]

            chain = select(0)

            def he_lo(r1):
                for k in range(KB):
                    if k % 4 == 0:
                        ve.wait_ge(he_hi_done, r1 * KB - (KB - k - 4))
                    nc.vector.scalar_tensor_tensor(h_lo[:, k, 0:P], bank[6 + k // 4][:, (k % 4) * P:(k % 4 + 1) * P],
                                                   g_col[:, 48 + k:49 + k], h_hi[:, k, 0:P].bitcast(f32),
                                                   ALU.mult, ALU.subtract).then_inc(he_lo_done, 1)

            he_lo(1)
            nc.vector.memset(y[:, :, :], 0.0).then_inc(acc_done, 1)
            ve.wait_ge(rtab_done, 1)
            rounds = ve.value_load(rtab_i[0:1, 0:1], min_val=E, max_val=E + X_ROUNDS)
            with ve.Fori(0, rounds) as r:
                def lo_e(j):
                    split_lo((MOE_U0 + j) % SPLIT_SLOTS, (MOE_U0 + j) % RAW_SLOTS, r * ROUND_UNITS + (MOE_U0 + j + 1))

                def used(j):
                    return r * ROUND_UNITS + (MOE_U0 + j + 1)

                q0 = r * N_EG + N_FG
                for j in range(6):
                    lo_e(j)
                gated(q0 + 1, used(j_up(0) + 1))
                for g in range(N_EG):
                    if g < N_EG - 1:
                        if g > 0:
                            lo_e(j_gate(g + 1))
                            lo_e(j_gate(g + 1) + 1)
                        lo_e(j_up(g + 1))
                        lo_e(j_up(g + 1) + 1)
                        aT_low(q0 + (g + 1))
                        lo_e(j_down(g))
                        lo_e(j_down(g) + 1)
                        gated(q0 + (g + 2), used(j_up(g + 1) + 1))
                    else:
                        lo_e(j_down(g))
                        lo_e(j_down(g) + 1)
                        aT_low(q0 + (g + 1))
                    if g == 2:
                        ve.wait_ge(gT_psum, r + 1)
                        ve.wait_ge(sel_done, r + 1)
                        assert select(r * chain + chain) == chain
                he_lo(r + 2)
                ve.wait_ge(unit_used, used(ROUND_UNITS - 1))
                ve.wait_ge(sc_psum, r)
                nc.vector.tensor_copy(ye[:, HALF:D], bank[5][:, :]).then_inc(ye_dve, 1)
                ve.wait_ge(sc_psum, r + 1)
                ve.wait_ge(acc_done, r * 4 + 1)
                for tb in range(TB):
                    for half in range(2):
                        cols = slice(half * HALF, (half + 1) * HALF)
                        nc.vector.tensor_tensor(y[:, tb, cols], y[:, tb, cols], bank[4 + 2 * tb + half][:, :],
                                                ALU.add).then_inc(acc_done, 1)
            ve.wait_ge(acc_done, rounds * 4 + 1)
            add_normed(7, lambda tb, half: y[:, tb, half * HALF:(half + 1) * HALF], 0, 48)

        @block.tensor
        def _(pe):
            mm = nc.tensor.matmul

            def three(out, a_hi, a_lo, b_hi, b_lo, first, last):
                mm(out, a_hi, b_hi, start=first, stop=False)
                mm(out, a_hi, b_lo, start=False, stop=False)
                return mm(out, a_lo, b_hi, start=False, stop=last)

            def weights(u, n):
                s = u % SPLIT_SLOTS
                pe.wait_ge(lo_ready, u + 1)
                return part(w_hi, s, n), part(w_lo, s, n)

            def input_transposed(phase):
                for tb in range(TB):
                    pe.wait_ge(xn_done, 2 * phase + tb + 1)
                for b in range(4):
                    for i in range(2):
                        for tb in range(TB):
                            c = (2 * b + i) * P
                            step = nc.tensor.transpose(bank[b][:, i * T + tb * P:i * T + (tb + 1) * P],
                                                       xn[:, tb, c:c + P], ident)
                    step.then_inc(tr_done, 1)

            pe.wait_ge(consts_in, 16)
            pe.wait_ge(grows_in, 16)
            nc.tensor.transpose(bank[7][:, 0:64], g_rows[:, :], consts[0:64, 0:64]).then_inc(gcol_psum, 1)
            pe.wait_ge(bands_in, 16)
            for tb in range(TB):
                pe.wait_ge(xn_done, tb + 1)
            for k in range(KB):
                at = bank[k // 2]
                c = (k % 2) * T
                mm(at[:, c:c + T], xn[:, 0, k * P:(k + 1) * P], bands[:, k // 2, 0:T], start=True, stop=False)
                step = mm(at[:, c + P:c + T], xn[:, 1, k * P:(k + 1) * P], bands[:, k // 2, T:T + P],
                          start=False, stop=True)
                if k % 2:
                    step.then_inc(tr_done, 1)
            pe.wait_ge(h_lo_done, KB)
            hi, lo = weights(0, FG)
            pe.wait_ge(gcol_done, 1)
            for tb in range(TB):
                tok = slice(tb * P, (tb + 1) * P)
                for g in range(POOL_G):
                    to = bank[4 + 2 * tb + g // 2][:, (g % 2) * FG:(g % 2 + 1) * FG]
                    for i in range(2):
                        k = 2 * g + i
                        step = three(to, h_hi[:, k, tok], h_lo[:, k, tok], hi[:, k, :], lo[:, k, :], i == 0, i == 1)
            step.then_inc(unit_used, 1)

            input_transposed(1)
            pe.wait_ge(h_lo_done, 2 * KB)

            def ffn_in(u, to):
                hi, lo = weights(u, FG)
                for tb in range(TB):
                    tok = slice(tb * P, (tb + 1) * P)
                    for k in range(KB):
                        step = three(to[:, tb * FG:(tb + 1) * FG], h_hi[:, k, tok], h_lo[:, k, tok],
                                     hi[:, k, :], lo[:, k, :], k == 0, k == KB - 1)
                step.then_inc(unit_used, 1)

            def transpose_act(q, sources):
                pe.wait_ge(act_done, q)
                pe.wait_ge(aT_lo_done, q - 1) if not isinstance(q, int) or q > 1 else None
                for i, source in enumerate(sources):
                    step = nc.tensor.transpose(bank[2][:, i * P:(i + 1) * P], source, ident)
                step.then_inc(aT_psum, 1)

            ffn_in(u_gate(0), bank[0])
            ffn_in(u_up(0), bank[1])
            pe.wait_ge(x_done, 2)
            for g in range(N_FG):
                if g < N_FG - 1:
                    pe.wait_ge(silu_done, g + 1)
                    ffn_in(u_gate(g + 1), bank[0])
                transpose_act(g + 1, [act[:, tb * FG + f * P:tb * FG + (f + 1) * P] for f in range(2) for tb in range(TB)])
                if g < N_FG - 1:
                    ffn_in(u_up(g + 1), bank[1])
                pe.wait_ge(aT_lo_done, g + 1)
                hi, lo = weights(u_down(g), D)
                for tb in range(TB):
                    for half in range(2):
                        cols = slice(half * HALF, (half + 1) * HALF)
                        for f in range(2):
                            tok = slice(f * T + tb * P, f * T + (tb + 1) * P)
                            step = three(bank[4 + 2 * tb + half][:, :], aT_hi[:, tok], aT_lo[:, tok],
                                         hi[:, f, cols], lo[:, f, cols], g == 0 and f == 0, g == N_FG - 1 and f == 1)
                step.then_inc(unit_used, 1)

            input_transposed(2)
            pe.wait_ge(h_lo_done, 3 * KB)
            pe.wait_ge(small_lo, 2)
            for tb in range(TB):
                tok = slice(tb * P, (tb + 1) * P)
                for k in range(KB):
                    mm(bank[6][:, tb * 2 * H:(tb + 1) * 2 * H], h_hi[:, k, tok], wf2[:, k, :], start=(k == 0), stop=False)
                    step = mm(bank[6][:, tb * 2 * H:(tb + 1) * 2 * H], h_lo[:, k, tok], wf2[:, k, :],
                              start=False, stop=(k == KB - 1))
            step.then_inc(f_psum, 1)

            def v_unit(i):
                hi, lo = weights(V_U0 + i, HALF)
                for tb in range(TB):
                    tok = slice(tb * P, (tb + 1) * P)
                    for k in range(4):
                        kb = 4 * (i % 2) + k
                        step = three(bank[4 + 2 * (i // 2) + tb][:, :], h_hi[:, kb, tok], h_lo[:, kb, tok],
                                     hi[:, k, :], lo[:, k, :], kb == 0, kb == KB - 1)
                step.then_inc(unit_used, 1)

            v_unit(0)
            v_unit(1)
            pe.wait_ge(logf_done, 1)
            mm(bank[3][0:H, 0:T], logf[:, 0, :], consts[:, C_TRI:C_TRI + T], start=True, stop=False)
            mm(bank[3][0:H, P:T], logf[:, 1, :], consts[:, C_TRI:C_TRI + P], start=False, stop=True).then_inc(c_psum, 1)
            v_unit(2)
            v_unit(3)

            def head_outputs(j):
                for i in range(2):
                    pe.wait_ge(p_done, 2 * j + i + 1)
                    if j > 0:
                        pe.wait_ge(pT_done, 2 * (j - 1) + i + 1)
                    nc.tensor.transpose(bank[4 + i][:, 0:P], logit[:, i, 0:P], ident)
                    nc.tensor.transpose(bank[4 + i][:, P:2 * P], logit[:, i, P:2 * P], ident)
                    nc.tensor.transpose(bank[4 + i][:, 2 * P:3 * P], logit[:, i, 2 * P:3 * P], ident).then_inc(pT_psum, 1)
                if j > 0:
                    pe.wait_ge(o_lo_done, j)
                for i in range(2):
                    pe.wait_ge(pT_done, 2 * j + i + 1)
                    c = (2 * j + i) * HD
                    to = bank[6][i * HD:(i + 1) * HD, :]
                    mm(to[:, 0:T], v[:, 0, c:c + HD], pT[:, i, 0:T], start=True, stop=False)
                    step = mm(to[:, P:T], v[:, 1, c:c + HD], pT[:, i, T:3 * P], start=False, stop=True)
                step.then_inc(o_psum, 1)

            for j in range(H // 2):
                hi, lo = weights(QK_U0 + j, T)
                if j == 0:
                    pe.wait_ge(v_done, 4)
                    pe.wait_ge(heads_in, 16)
                    pe.wait_ge(ncT_done, 1)
                for i in range(2):
                    for k in range(KB):
                        cols = slice(i * P, (i + 1) * P)
                        step = three(bank[0][:, i * T:(i + 1) * T], hi[:, k, cols], lo[:, k, cols],
                                     h_hi[:, k, :], h_lo[:, k, :], k == 0, k == KB - 1)
                step.then_inc(unit_used, 1)
                if j > 0:
                    head_outputs(j - 1)
                pe.wait_ge(q_done, j + 1)
                pe.wait_ge(k_done, j + 1)
                for i in range(2):
                    if j > 0:
                        pe.wait_ge(mx_done, 2 * (j - 1) + i + 1)
                    h0 = i * HD
                    for b in range(TB):
                        to = bank[1 + i][:, b * P:b * P + (b + 1) * P]
                        mm(to, qk[h0:h0 + HD, b * P:(b + 1) * P], qk[h0:h0 + HD, T:T + (b + 1) * P],
                           start=True, stop=False)
                        step = mm(to, head_row[:, 2 * j + i, :], ncT[:, 0:(b + 1) * P], start=False, stop=True)
                    step.then_inc(s_psum, 1)
            head_outputs(H // 2 - 1)
            pe.wait_ge(o_lo_done, H // 2)
            pe.wait_ge(mx_done, H)
            for w in range(4):
                hi, lo = weights(OUT_U0 + w, D)
                for tb in range(TB):
                    tok = slice(tb * P, (tb + 1) * P)
                    for half in range(2):
                        cols = slice(half * HALF, (half + 1) * HALF)
                        for i in range(2):
                            k = 2 * w + i
                            step = three(bank[(1, 2, 3, 7)[2 * tb + half]][:, :], o_hi[:, k, tok], o_lo[:, k, tok],
                                         hi[:, i, cols], lo[:, i, cols], k == 0, k == KB - 1)
                step.then_inc(unit_used, 1)

            pe.wait_ge(x_done, 6)
            input_transposed(3)
            pe.wait_ge(h_lo_done, 4 * KB)
            for tb in range(TB):
                tok = slice(tb * P, (tb + 1) * P)
                for k in range(KB):
                    mm(bank[4][:, tb * 2 * E:(tb + 1) * 2 * E], h_hi[:, k, tok], wr2[:, k, :], start=(k == 0), stop=False)
                    step = mm(bank[4][:, tb * 2 * E:(tb + 1) * 2 * E], h_lo[:, k, tok], wr2[:, k, :],
                              start=False, stop=(k == KB - 1))
            step.then_inc(lg_psum, 1)
            pe.wait_ge(m_done, 1)
            ones, before = consts[:, C_ONES:C_ONES + P], consts[:, C_TRIS:C_TRIS + P]
            mm(bank[5][:, 0:E], before, mboth[:, 0, :], start=True, stop=True)
            mm(bank[5][:, E:2 * E], ones, mboth[:, 0, :], start=True, stop=False)
            mm(bank[5][:, E:2 * E], before, mboth[:, 1, :], start=False, stop=True)
            mm(bank[5][:, 2 * E:3 * E], ones, mboth[:, 0, :], start=True, stop=False)
            mm(bank[5][:, 2 * E:3 * E], ones, mboth[:, 1, :], start=False, stop=True).then_inc(rank_psum, 1)

            def gather(r1):
                pe.wait_ge(sel_done, r1)
                for k in range(KB):
                    for tb in range(TB):
                        step = mm(bank[6 + k // 4][:, (k % 4) * P:(k % 4 + 1) * P], xn[:, tb, k * P:(k + 1) * P],
                                  sel[:, tb, :], start=(tb == 0), stop=(tb == 1))
                step.then_inc(he_psum, 1)

            gather(1)
            pe.wait_ge(rtab_done, 1)
            rounds = pe.value_load(rtab_i[0:1, 0:1], min_val=E, max_val=E + X_ROUNDS)
            with pe.Fori(0, rounds) as r:
                def weights_e(j, n):
                    s = (MOE_U0 + j) % SPLIT_SLOTS
                    pe.wait_ge(lo_ready, r * ROUND_UNITS + (MOE_U0 + j + 1))
                    return part(w_hi, s, n), part(w_lo, s, n)

                def expert_in(j, to):
                    for i in range(2):
                        hi, lo = weights_e(j + i, HALF)
                        for k in range(4):
                            kb = 4 * i + k
                            step = three(to[:, :], h_hi[:, kb, 0:P], h_lo[:, kb, 0:P], hi[:, k, :], lo[:, k, :],
                                         kb == 0, kb == KB - 1)
                        step.then_inc(unit_used, 1)

                q0 = r * N_EG + N_FG
                pe.wait_ge(he_lo_done, r * KB + KB)
                pe.wait_ge(silu_done, q0)
                expert_in(j_gate(0), bank[0])
                pe.wait_ge(act_done, q0)
                expert_in(j_up(0), bank[1])
                pe.wait_ge(sel_done, r + 1)
                for tb in range(TB):
                    step = nc.tensor.transpose(bank[3][:, tb * P:(tb + 1) * P], gsel[:, tb, :], ident)
                step.then_inc(gT_psum, 1)
                for g in range(N_EG):
                    if g < N_EG - 1:
                        pe.wait_ge(silu_done, q0 + (g + 1))
                        expert_in(j_gate(g + 1), bank[0])
                    transpose_act(q0 + (g + 1), [act[:, f * P:(f + 1) * P] for f in range(4)])
                    if g < N_EG - 1:
                        expert_in(j_up(g + 1), bank[1])
                    else:
                        pe.wait_ge(acc_done, r * 4 + 1)
                        gather(r + 2)
                    pe.wait_ge(aT_lo_done, q0 + (g + 1))
                    if g == 0:
                        pe.wait_ge(acc_done, r * 4 + 1)
                    for i in range(2):
                        hi, lo = weights_e(j_down(g) + i, D)
                        for half in range(2):
                            cols = slice(half * HALF, (half + 1) * HALF)
                            for f in range(2):
                                blk = slice((2 * i + f) * P, (2 * i + f + 1) * P)
                                step = three(bank[4 + half][:, :], aT_hi[:, blk], aT_lo[:, blk], hi[:, f, cols],
                                             lo[:, f, cols], g == 0 and i == 0 and f == 0,
                                             g == N_EG - 1 and i == 1 and f == 1)
                        step.then_inc(unit_used, 1)
                pe.wait_ge(ye_act, r + 1)
                pe.wait_ge(ye_dve, r + 1)
                pe.wait_ge(gT_done, r + 1)
                pe.wait_ge(he_lo_done, r * KB + 2 * KB)
                for tb in range(TB):
                    for half in range(2):
                        step = mm(bank[4 + 2 * tb + half][:, :], gselT[:, tb * P:(tb + 1) * P],
                                  ye[:, half * HALF:(half + 1) * HALF], start=True, stop=True)
                step.then_inc(sc_psum, 1)

        @block.gpsimd
        def _(po):
            po.wait_ge(tr_done, 4)
            po.dma_start(head_row[:, :, :], heads_d).then_inc(heads_in, 16)


_INS = ["x", "norm_g", "pool_w", "pool_scale", "attn_w_in", "attn_b_f", "attn_w_out", "ffn_w_gate", "ffn_w_up",
        "ffn_w_down", "moe_w_router", "moe_w_gate", "moe_w_up", "moe_w_down"]


def _constants():
    s, t = np.arange(P)[:, None], np.arange(P)[None, :]
    c = np.zeros((P, C_ALL), np.float32)
    c[:, C_IDENT:C_IDENT + P] = s == t
    c[:, C_TRI:C_TRI + P] = s <= t
    c[:, C_ONES:C_ONES + P] = 1
    c[:, C_TRIS:C_TRIS + P] = s < t
    causal = np.where(t <= s, 0, NEG_INF)
    c[:, C_MASK:C_MASK + P] = causal
    c[:, C_MASK + 2 * P:C_MASK + 3 * P] = causal
    c[:, C_IOTA:C_IOTA + P] = t
    tok = np.arange(T)
    bands = np.zeros((P, POOL_G, 3 * P), np.float32)
    for g, w in enumerate(POOL_WINDOWS):
        full = ((tok[:, None] <= tok[None, :]) & (tok[:, None] > tok[None, :] - w)) / np.minimum(tok + 1, w)[None, :]
        full = full - np.eye(T)
        bands[:, g, 0:T] = full[0:P]
        bands[:, g, T:] = full[P:, P:]
    heads = np.zeros((H, H, P), np.float32)
    for h in range(H):
        heads[h, h, :] = 1
    return {"consts": c, "bands": bands, "heads": heads}


def kernel(**inputs):
    import concourse.bacc as bacc
    from concourse.bass_utils import run_bass_kernel_spmd

    nc = bacc.Bacc("TRN2", target_bir_lowering=False, num_devices=1)
    arrays, args = {}, []
    for name, a in [(n, np.ascontiguousarray(inputs[n])) for n in _INS] + list(_constants().items()):
        arrays[f"in_{name}"] = a
        args.append(nc.dram_tensor(f"in_{name}", a.shape, mybir.dt.from_np(a.dtype), kind="ExternalInput").ap())
    args.append(nc.dram_tensor("out_x", (1, T, D), mybir.dt.float32, kind="ExternalOutput").ap())
    trunk(nc, *args)
    result = run_bass_kernel_spmd(nc, [arrays], core_ids=[0])
    return result.results[0]["out_x"]
```

```python
from contextlib import ExitStack

import numpy as np

import concourse.bass as bass
from concourse import mybir

P = 128
D = 1024
KB = D // P
T = 256
TB = T // P
HALF = 512
POOL_WINDOWS = (2, 4, 8, 16)
POOL_G = len(POOL_WINDOWS)
H = 16
HD = D // H
LO_ROW = 64
F_DENSE = 2816
FG = 256
N_FG = F_DENSE // FG
E = 8
F_EXP = 3584
N_EG = F_EXP // HALF
EPS = 1e-6
NEG_INF = -1e30

UNIT = 2048
RAW_SLOTS = 7
EXTRA_SLOTS = 4
SPLIT_SLOTS = 3
FFN_U0 = 1
V_U0 = FFN_U0 + 3 * N_FG
QK_U0 = V_U0 + 4
OUT_U0 = QK_U0 + H // 2
MOE_U0 = OUT_U0 + 4
ROUND_UNITS = 6 * N_EG
EXPERT_RING = [*range(11), *range(10), *range(11), *range(9), 10]
assert len(EXPERT_RING) == ROUND_UNITS
SELECT_STEPS = 10
X_ROUNDS = 3

C_IDENT = 0
C_ONES = 128
C_TRIS = 256
C_MASK = 384
C_IOTA = 768
C_ALL = 896

WARM_START = 24
WARM = (56, 30, 10, 12, 28, 4)


def select(eng, ops, chain, before, gpos, gpos_next, slots_step, gate, sel, sel2, gsel, consts, ready,
           ready_count, done, ALU):
    iota = consts[:, C_IOTA:C_IOTA + P]
    ops.tensor_tensor(gpos_next[:, :, :], gpos[:, :, :], slots_step[:, :, :], ALU.subtract).then_inc(chain, 1)
    n = 1
    for tb in range(TB):
        for i, to in enumerate((sel, sel2)):
            ops.tensor_scalar(to[:, tb, :], iota, gpos[:, tb, i:i + 1], None, ALU.is_equal).then_inc(chain, 1)
            n += 1
    eng.wait_ge(chain, before + n)
    for tb in range(TB):
        ops.tensor_tensor(gsel[:, tb, :], sel[:, tb, :], gate[:, tb, 0:1].to_broadcast([P, P]),
                          ALU.mult).then_inc(chain, 1)
        n += 1
    eng.wait_ge(chain, before + n)
    ops.tensor_tensor(sel[:, :, :], sel[:, :, :], sel2[:, :, :], ALU.add).then_inc(ready, 1)
    eng.wait_ge(ready, ready_count)
    for tb in range(TB):
        ops.tensor_tensor(sel2[:, tb, :], sel2[:, tb, :], gate[:, tb, 1:2].to_broadcast([P, P]),
                          ALU.mult).then_inc(chain, 1)
        n += 1
    eng.wait_ge(chain, before + n)
    ops.tensor_tensor(gsel[:, :, :], gsel[:, :, :], sel2[:, :, :], ALU.add).then_inc(chain, 1)
    n += 1
    ops.tensor_scalar(gpos[:, :, :], gpos_next[:, :, :], 0.0, None, ALU.add).then_inc(done, 1)
    return n


def trunk(nc, x_d, norm_g, pool_w, pool_scale, w_in, b_f, w_out, ffn_gate, ffn_up, ffn_down,
          w_router, moe_gate, moe_up, moe_down, consts_d, bands_d, heads_d, out_d):
    f32 = mybir.dt.float32
    f32r = mybir.dt.float32r
    i32 = mybir.dt.int32
    u32 = mybir.dt.uint32
    ALU = mybir.AluOpType
    ACT = mybir.ActivationFunctionType
    AX = mybir.AxisListType

    with ExitStack() as ctx:
        def sb(name, shape, dt=f32):
            return ctx.enter_context(nc.sbuf_tensor(name, shape, dt))

        def sem(name):
            return ctx.enter_context(nc.semaphore(name))

        raw = sb("raw", [P, RAW_SLOTS, UNIT])
        w_hi = sb("w_hi", [P, SPLIT_SLOTS, UNIT], f32r)
        w_lo = sb("w_lo", [P, SPLIT_SLOTS, UNIT], f32r)
        x = sb("x", [P, TB, D])
        xn = sb("xn", [P, TB, D])
        h_hi = sb("h_hi", [P, KB, T], f32r)
        h_lo = sb("h_lo", [P, KB, T], f32r)
        with nc.sbuf_tensor("o_hi", [P, KB, T], f32r) as o_hi:
            pass
        y = sb("y", [P, TB, D])
        gain = sb("gain", [P, 2, D])
        consts = sb("consts", [P, C_ALL])
        sums = sb("sums", [P, 8, TB, 2])
        root_t = sb("root_t", [P, 5, TB])
        rstd = sb("rstd", [P, 8, TB])
        silu = sb("silu", [P, HALF])
        act = sb("act", [P, HALF])
        aT_hi = sb("aT_hi", [P, HALF], f32r)
        aT_lo = sb("aT_lo", [P, HALF], f32r)
        small_w = sb("small_w", [P, KB, H + E])
        wf2 = sb("wf2", [P, KB, 2 * H], f32r)
        wr2 = sb("wr2", [P, KB, 2 * E], f32r)
        bf = sb("bf", [H, 1])
        with nc.sbuf_tensor("bands", [P, POOL_G, 3 * P], f32) as bands, \
                nc.sbuf_tensor("scale", [P, D], f32) as scale:
            pass
        with ExitStack() as attn:
            def sa(name, shape, dt=f32):
                return attn.enter_context(nc.sbuf_tensor(name, shape, dt))
            qk = sa("qk", [P, 2 * T])
            logit = sa("logit", [P, 2, 3 * P])
            pT = sa("pT", [P, 2, 3 * P])
            fz = sa("fz", [H, T])
            fe = sa("fe", [H, T])
            fl = sa("fl", [H, T])
            ncT = sa("ncT", [H, T])
            ncT2 = sa("ncT2", [LO_ROW + H, T], f32r)
            mx = sa("mx", [P, H // 2, 4])
            nmx = sa("nmx", [P, H // 2, 4])
            den = sa("den", [P, H // 2, 4])
            rden = sa("rden", [P, H // 2, 4])
            head_row = sa("head_row", [LO_ROW + H, H, P], f32r)
            o_lo = sa("o_lo", [P, KB, T], f32r)
            v = sa("v", [P, TB, D])
        ye = sb("ye", [P, D])
        sel = sb("sel", [P, TB, P])
        gsel = sb("gsel", [P, TB, P])
        gselT = sb("gselT", [P, T])
        sel2 = sb("sel2", [P, TB, P])
        lg = sb("lg", [P, TB, E])
        top = sb("top", [P, TB, 8])
        topi = sb("topi", [P, TB, 8], u32)
        topf = sb("topf", [P, TB, 2])
        gate = sb("gate", [P, TB, 2])
        gtmp = sb("gtmp", [P, TB, 3])
        m12 = sb("m12", [P, TB, 2, E])
        mboth = sb("mboth", [P, TB, E])
        rank = sb("rank", [P, TB, E])
        over = sb("over", [P, TB, E])
        prod = sb("prod", [P, TB, 2, E])
        gpos = sb("gpos", [P, TB, 2])
        gpos_next = sb("gpos_next", [P, TB, 2])
        slots_step = sb("slots_step", [P, TB, 2])
        ctab = sb("ctab", [P, 8, E])
        rtab = sb("rtab", [1, 4])
        rtab_i = sb("rtab_i", [1, 4], i32)
        raw_extra = sb("raw_extra", [P, EXTRA_SLOTS, UNIT])
        bank = [ctx.enter_context(nc.psum_tensor(f"bank{i}", [P, HALF], f32)) for i in range(8)]

        ident = consts[:, C_IDENT:C_IDENT + P]
        lgT = act[0:E, 0:T]

        raw_in = [sem(f"raw_in{i}") for i in range(RAW_SLOTS + EXTRA_SLOTS)]
        hi_ready = sem("hi_ready")
        lo_ready = sem("lo_ready")
        unit_used = sem("unit_used")
        x_in = [sem("x_in0"), sem("x_in1")]
        consts_in = sem("consts_in")
        bands_in = sem("bands_in")
        ones_done = sem("ones_done")
        heads_in = sem("heads_in")
        small_in = sem("small_in")
        gain_first = [sem("gain_first0"), sem("gain_first1")]
        gain_in = [sem("gain_in0"), sem("gain_in1")]
        out_in = sem("out_in")
        sq_done = sem("sq_done")
        dve = sem("dve")
        xn_done = sem("xn_done")
        tr_done = sem("tr_done")
        h_hi_done = sem("h_hi_done")
        h_lo_done = sem("h_lo_done")
        y0_psum = sem("y0_psum")
        y_done = sem("y_done")
        scale_in = sem("scale_in")
        yg_done = sem("yg_done")
        x_done = sem("x_done")
        silu_done = sem("silu_done")
        act_done = sem("act_done")
        aT_psum = sem("aT_psum")
        aT_hi_done = sem("aT_hi_done")
        aT_lo_done = sem("aT_lo_done")
        small_hi = sem("small_hi")
        small_lo = sem("small_lo")
        f_psum = sem("f_psum")
        fz_done = sem("fz_done")
        fe_done = sem("fe_done")
        fl_done = sem("fl_done")
        ncT_done = sem("ncT_done")
        v_done = sem("v_done")
        q_done = sem("q_done")
        k_done = sem("k_done")
        s_psum = sem("s_psum")
        mx_done = sem("mx_done")
        exp_done = sem("exp_done")
        p_done = sem("p_done")
        pT_psum = sem("pT_psum")
        pT_done = sem("pT_done")
        o_psum = sem("o_psum")
        o_hi_done = sem("o_hi_done")
        o_lo_done = sem("o_lo_done")
        lgT_psum = sem("lgT_psum")
        lgT_done = sem("lgT_done")
        lg_psum = sem("lg_psum")
        gap_done = sem("gap_done")
        gexp_done = sem("gexp_done")
        m_done = sem("m_done")
        rank_psum = sem("rank_psum")
        rtab_done = sem("rtab_done")
        sel_done = sem("sel_done")
        gT_psum = sem("gT_psum")
        gT_done = sem("gT_done")
        he_psum = sem("he_psum")
        he_hi_done = sem("he_hi_done")
        he_lo_done = sem("he_lo_done")
        ye_act = sem("ye_act")
        ye_dve = sem("ye_dve")
        sc_psum = sem("sc_psum")
        acc_done = sem("acc_done")
        pool_scaled = sem("pool_scaled")
        sel_ready = sem("sel_ready")
        pool_step = sem("pool_step")

        landed, on_slot = [], [0] * RAW_SLOTS
        for u in range(MOE_U0):
            on_slot[u % RAW_SLOTS] += 32 if QK_U0 <= u < OUT_U0 else 16
            landed.append(on_slot[u % RAW_SLOTS])


        def moe_slot(j):
            place = EXPERT_RING[j % ROUND_UNITS]
            return (MOE_U0 + place) % RAW_SLOTS if place < RAW_SLOTS else place

        def moe_landed(r, j):
            s, places = moe_slot(j), [moe_slot(i) for i in range(ROUND_UNITS)]
            here = 16 * places.count(s)
            before = on_slot[s] if s < RAW_SLOTS else 0
            upto = places[:j % ROUND_UNITS + 1].count(s)
            return r * here + (before + here * (j // ROUND_UNITS) + 16 * upto)

        def moe_last(j):
            return max(i for i in range(j - ROUND_UNITS, j) if moe_slot(i) == moe_slot(j))

        def raw_slot(s):
            return raw[:, s, :] if s < RAW_SLOTS else raw_extra[:, s - RAW_SLOTS, :]

        landed += [moe_landed(0, j) for j in range(SPLIT_SLOTS)]

        def u_gate(g):
            return FFN_U0 + (0 if g == 0 else 3 * g - 1 + 0)

        def u_up(g):
            return u_gate(g) + 1

        def u_down(g):
            return FFN_U0 + (3 * g + 4 if g < N_FG - 1 else 3 * g + 2)

        def j_gate(g):
            return 0 if g == 0 else 6 * g - 2

        def j_up(g):
            return j_gate(g) + 2

        def j_down(g):
            return 6 * g + 8 if g < N_EG - 1 else 6 * g + 4

        def sq_at(n, tb):
            if n == 0:
                return tb + 1
            if n == 7:
                return 20 + 2 * tb + 2
            before, pre = 2 + 6 * ((n - 1) // 2), n % 2 == 0
            if n in (3, 4):
                return before + (4 + tb + 1 if pre else 2 * tb + 2)
            return before + 3 * tb + (3 if pre else 2)

        def slot_of(u):
            return u % RAW_SLOTS if u < MOE_U0 else moe_slot(u - MOE_U0)

        def blocks_of(slot, n):
            return slot.rearrange("p (b n) -> p b n", n=n)

        def part(t, s, n):
            return blocks_of(t[:, s, :], n)

        def input_part(t, phase, b):
            if phase == 0:
                return t[:, 2 * b:2 * b + 2, :]
            return t[:, 4 * (b % 2):4 * (b % 2) + 4, (b // 2) * P:(b // 2 + 1) * P]

        def bank_blocks(phase, b):
            return bank[b][:, :].rearrange("p (b n) -> p b n", n=T if phase == 0 else P)

        block = ctx.enter_context(nc.Block())

        @block.sync
        def _(sp):
            def rows(w, first, blocks, col, n):
                return w[first * P:(first + blocks) * P, col:col + n].rearrange("(b p) n -> p b n", p=P)

            def load(u, src, n):
                if u >= RAW_SLOTS:
                    sp.wait_ge(lo_ready, u - RAW_SLOTS + 1)
                sp.dma_start(part(raw, u % RAW_SLOTS, n), src).then_inc(raw_in[u % RAW_SLOTS], 16)

            for tb in range(TB):
                sp.dma_start(x[:, tb, :], x_d[0, tb * P:(tb + 1) * P, :]).then_inc(x_in[tb], 16)
            sp.dma_start(gain[:, 0, :], norm_g[0, 0:1, :].to_broadcast([P, D])).then_inc(gain_first[0], 16)
            sp.dma_start(bands[:, :, :], bands_d).then_inc(bands_in, 16)
            load(0, pool_w[0].rearrange("g (b p) n -> p (g b) n", p=P), FG)
            sp.dma_start(scale[:, :], pool_scale.to_broadcast([P, D])).then_inc(scale_in, 16)
            sp.dma_start(gain[:, 1, :], norm_g[0, 1:2, :].to_broadcast([P, D])).then_inc(gain_first[1], 16)
            sp.dma_start(consts[:, :], consts_d).then_inc(consts_in, 16)
            load(1, rows(ffn_gate[0], 0, KB, 0, FG), FG)
            load(2, rows(ffn_up[0], 0, KB, 0, FG), FG)
            sp.dma_start(small_w[:, :, 0:H],
                         w_in[0, :, 3 * D:3 * D + H].rearrange("(k p) n -> p k n", p=P)).then_inc(small_in, 16)
            sp.dma_start(small_w[:, :, H:H + E],
                         w_router[0].rearrange("(k p) n -> p k n", p=P)).then_inc(small_in, 16)
            sp.dma_start(bf[:, :], b_f.rearrange("o h -> h o")).then_inc(small_in, 16)
            for u in range(FFN_U0 + 2, V_U0):
                for g in range(N_FG):
                    if u == u_gate(g):
                        load(u, rows(ffn_gate[0], 0, KB, g * FG, FG), FG)
                    elif u == u_up(g):
                        load(u, rows(ffn_up[0], 0, KB, g * FG, FG), FG)
                    elif u == u_down(g):
                        load(u, rows(ffn_down[0], 2 * g, 2, 0, D), D)
            for i in range(4):
                load(V_U0 + i, rows(w_in[0], 4 * (i % 2), 4, 2 * D + (i // 2) * HALF, HALF), HALF)
            for j in range(H // 2):
                u = QK_U0 + j
                sp.wait_ge(lo_ready, u - RAW_SLOTS + 1)
                for i in range(2):
                    sp.dma_start(part(raw, u % RAW_SLOTS, T)[:, :, i * P:(i + 1) * P],
                                 rows(w_in[0], 0, KB, i * D + j * P, P)).then_inc(raw_in[u % RAW_SLOTS], 16)
            for i in range(4):
                load(OUT_U0 + i, rows(w_out[0], 2 * i, 2, 0, D), D)

            def expert(r, e):
                gate_e = moe_gate[0, bass.ds(e, 1), :, :].rearrange("a k n -> (a k) n")
                up_e = moe_up[0, bass.ds(e, 1), :, :].rearrange("a k n -> (a k) n")
                down_e = moe_down[0, bass.ds(e, 1), :, :].rearrange("a k n -> (a k) n")

                def load_e(j, src, n):
                    s = moe_slot(j)
                    sp.wait_ge(lo_ready, r * ROUND_UNITS + (MOE_U0 + moe_last(j) + 1))
                    if moe_last(j) < 0:
                        place = EXPERT_RING[j]
                        sp.wait_ge(*([(lo_ready, MOE_U0 - RAW_SLOTS + place + 1)] if place < RAW_SLOTS else
                                     [(unit_used, OUT_U0 + 1), (unit_used, MOE_U0), (x_done, 6), (x_done, 6)][place - RAW_SLOTS:])[0])
                    sp.dma_start(blocks_of(raw_slot(s), n), src).then_inc(raw_in[s], 16)

                for g in range(-1, N_EG):
                    for i in range(2):
                        if g < N_EG - 1:
                            load_e(j_gate(g + 1) + i, rows(gate_e, 4 * i, 4, (g + 1) * HALF, HALF), HALF)
                    for i in range(2):
                        if g < N_EG - 1:
                            load_e(j_up(g + 1) + i, rows(up_e, 4 * i, 4, (g + 1) * HALF, HALF), HALF)
                    for i in range(2):
                        if g >= 0:
                            load_e(j_down(g) + i, rows(down_e, 4 * g + 2 * i, 2, 0, D), D)

            with sp.Fori(0, E) as r:
                expert(r, r)
            sp.wait_ge(rtab_done, 1)
            rounds = sp.value_load(rtab_i[0:1, 0:1], min_val=E, max_val=E + X_ROUNDS)
            for i in range(X_ROUNDS):
                e_x = sp.value_load(rtab_i[0:1, 1 + i:2 + i], min_val=0, max_val=E - 1)
                with sp.If(rounds > E + i):
                    expert(E + i, e_x)
            for tb in range(TB):
                for half in range(2):
                    cols = slice(half * HALF, (half + 1) * HALF)
                    sp.wait_ge(x_done, 2 * 3 + 2 * tb + half + 1)
                    sp.dma_start(out_d[0, tb * P:(tb + 1) * P, cols], x[:, tb, cols]).then_inc(out_in, 16)
            sp.wait_ge(out_in, 16 * 2 * TB)

        @block.scalar
        def _(sc):
            def split_hi(slot, source, arrived, used):
                sc.wait_ge(raw_in[source], arrived)
                if used is not None:
                    sc.wait_ge(unit_used, used)
                nc.scalar.activation(w_hi[:, slot, :], raw_slot(source), ACT.Copy).then_inc(hi_ready, 1)

            def hi(u):
                split_hi(u % SPLIT_SLOTS, slot_of(u), landed[u],
                         u - SPLIT_SLOTS + 1 if u >= SPLIT_SLOTS else None)

            def squares(n, tb):
                if n:
                    sc.wait_ge(x_done, n - 2 + tb + 1)
                nc.scalar.activation(xn[:, tb, :], x[:, tb, :], ACT.Square,
                                     accum_out=sums[:, n, tb, 0:1]).then_inc(sq_done, 1)

            def post_squares(n, tb, source, ready, squared, after=None):
                sc.wait_ge(*ready)
                for half in range(2):
                    if half == 1 and after is not None:
                        sc.wait_ge(yg_done, after)
                    nc.scalar.activation(squared(tb, half), source(tb, half), ACT.Square,
                                         accum_out=sums[:, n, tb, half:half + 1]).then_inc(sq_done, 1)

            def in_xn(tb, half):
                return xn[:, tb, half * HALF:(half + 1) * HALF]

            def in_v(tb, half):
                return v[:, tb, half * HALF:(half + 1) * HALF]

            def in_bank(tb, half):
                return bank[2 * tb + half][:, :]

            def in_y(tb, half):
                return y[:, tb, half * HALF:(half + 1) * HALF]

            def input_hi(phase, blocks=range(TB)):
                for b in [2 * tb + i for tb in blocks for i in range(2)]:
                    sc.wait_ge(tr_done, 4 * phase + b + 1)
                    nc.scalar.activation(input_part(h_hi, phase, b), bank_blocks(phase, b),
                                         ACT.Copy).then_inc(h_hi_done, 1)

            for tb in range(TB):
                sc.wait_ge(x_in[tb], 16)
                squares(0, tb)
            hi(0)
            input_hi(0)
            hi(1)
            hi(2)
            post_squares(1, 0, in_y, (y_done, 2), in_v)
            squares(2, 0)
            post_squares(1, 1, in_y, (y_done, 4), in_v)
            input_hi(1, [0])
            squares(2, 1)
            input_hi(1, [1])
            sc.wait_ge(small_in, 48)
            nc.scalar.activation(wf2[:, :, 0:H], small_w[:, :, 0:H], ACT.Copy).then_inc(small_hi, 1)
            nc.scalar.activation(wr2[:, :, 0:E], small_w[:, :, H:H + E], ACT.Copy).then_inc(small_hi, 1)

            def silu_group(q, used):
                sc.wait_ge(unit_used, used)
                if q is not None:
                    sc.wait_ge(act_done, q)
                nc.scalar.activation(silu[:, :], bank[0][:, :], ACT.Silu).then_inc(silu_done, 1)

            def aT_high(q):
                sc.wait_ge(aT_psum, q)
                nc.scalar.activation(aT_hi[:, :], bank[2][:, :],
                                     ACT.Copy).then_inc(aT_hi_done, 1)

            hi(3)
            silu_group(None, u_gate(0) + 1)
            for g in range(N_FG):
                if g < N_FG - 1:
                    hi(u_up(g + 1))
                    hi(u_down(g))
                    silu_group(g + 1, u_gate(g + 1) + 1)
                    if g > 0:
                        sc.wait_ge(unit_used, u_down(g - 1) + 1)
                    aT_high(g + 1)
                    hi(u_down(g) + 1)
                else:
                    hi(V_U0)
                    sc.wait_ge(unit_used, u_down(g - 1) + 1)
                    aT_high(g + 1)
                    hi(V_U0 + 1)
            def ffn_out(tb, half):
                return bank[4 + 2 * tb + half][:, :]

            post_squares(3, 0, ffn_out, (y0_psum, 2), in_xn, after=3)
            post_squares(3, 1, ffn_out, (unit_used, V_U0), in_xn)
            squares(4, 0)
            input_hi(2, [0])
            squares(4, 1)
            input_hi(2, [1])
            hi(V_U0 + 2)
            hi(V_U0 + 3)
            hi(QK_U0)
            sc.wait_ge(fz_done, 1)
            nc.scalar.activation(fe[:, :], fe[:, :], ACT.Exp, scale=-1.0).then_inc(fe_done, 1)
            sc.wait_ge(fe_done, 1)
            nc.scalar.activation(fl[:, :], fe[:, :], ACT.Ln, bias=1.0).then_inc(fl_done, 1)
            for half in range(2):
                sc.wait_ge(unit_used, V_U0 + 2 * half + 2)
                for tb in range(TB):
                    nc.scalar.activation(v[:, tb, half * HALF:(half + 1) * HALF], bank[4 + 2 * half + tb][:, :],
                                         ACT.Copy).then_inc(v_done, 1)
                if half == 0:
                    hi(QK_U0 + 1)

            def pT_copy(j):
                for i in range(2):
                    sc.wait_ge(pT_psum, 2 * j + i + 1)
                    if j > 0:
                        sc.wait_ge(o_psum, j)
                    nc.scalar.activation(pT[:, i, :], bank[4 + i][:, 0:3 * P], ACT.Copy).then_inc(pT_done, 1)

            def out_hi(j):
                sc.wait_ge(o_psum, j + 1)
                nc.scalar.activation(o_hi[:, j, :], bank[6][:, 0:T], ACT.Copy).then_inc(o_hi_done, 1)

            for j in range(H // 2):
                hi(QK_U0 + j + 2)
                sc.wait_ge(unit_used, QK_U0 + j + 1)
                if j > 0:
                    sc.wait_ge(s_psum, 2 * j)
                nc.scalar.activation(qk[:, 0:T], bank[0][:, 0:T], ACT.Copy, scale=HD ** -0.5).then_inc(q_done, 1)
                if j > 0:
                    pT_copy(j - 1)
                    out_hi(j - 1)
                for i in range(2):
                    for b in range(TB):
                        sc.wait_ge(mx_done, 2 * j + i + 1)
                        nc.scalar.activation(logit[:, i, b * P:(2 * b + 1) * P], logit[:, i, b * P:(2 * b + 1) * P],
                                             ACT.Exp, bias=nmx[:, j, 2 * i + b:2 * i + b + 1],
                                             accum_out=den[:, j, 2 * i + b:2 * i + b + 1]).then_inc(exp_done, 1)
            pT_copy(H // 2 - 1)
            out_hi(H // 2 - 1)
            for i in range(2):
                hi(OUT_U0 + 2 + i)
            def attn_out(tb, half):
                return bank[(1, 2, 3, 7)[2 * tb + half]][:, :]

            post_squares(5, 0, attn_out, (y0_psum, 3), in_xn, after=7)
            squares(6, 0)
            post_squares(5, 1, attn_out, (unit_used, MOE_U0), in_xn, after=9)
            input_hi(3, [0])
            squares(6, 1)
            input_hi(3, [1])
            for j in range(3):
                hi(MOE_U0 + j)
            sc.wait_ge(gap_done, 1)
            nc.scalar.activation(gtmp[:, :, 1:2], gtmp[:, :, 0:1], ACT.Exp).then_inc(gexp_done, 1)

            def he_hi(r1):
                for i in range(2):
                    sc.wait_ge(he_psum, r1 * 2 - (1 - i))
                    nc.scalar.activation(h_hi[:, 4 * i:4 * i + 4, 0:P], bank_blocks(3, 6 + i),
                                         ACT.Copy).then_inc(he_hi_done, 1)

            he_hi(1)
            sc.wait_ge(rtab_done, 1)
            rounds = sc.value_load(rtab_i[0:1, 0:1], min_val=E, max_val=E + X_ROUNDS)
            with sc.Fori(0, rounds) as r:
                def hi_e(j):
                    split_hi((MOE_U0 + j) % SPLIT_SLOTS, moe_slot(j), moe_landed(r, j),
                             r * ROUND_UNITS + (MOE_U0 + j - SPLIT_SLOTS + 1))

                def used(j):
                    return r * ROUND_UNITS + (MOE_U0 + j + 1)

                q0 = r * N_EG + N_FG
                hi_e(3)
                silu_group(q0, used(j_gate(0) + 1))
                for g in range(N_EG):
                    if g < N_EG - 1:
                        for j in range(j_gate(g + 1), j_gate(g + 1) + 4):
                            hi_e(j)
                        if g == 0:
                            sc.wait_ge(gT_psum, r + 1)
                            nc.scalar.activation(gselT[:, :], bank[3][:, 0:T], ACT.Copy).then_inc(gT_done, 1)
                        silu_group(q0 + (g + 1), used(j_gate(g + 1) + 1))
                        if g > 0:
                            sc.wait_ge(unit_used, used(j_down(g - 1) + 1))
                        aT_high(q0 + (g + 1))
                        hi_e(j_down(g))
                        hi_e(j_down(g) + 1)
                    else:
                        hi_e(j_down(g))
                        hi_e(j_down(g) + 1)
                        sc.wait_ge(unit_used, used(j_down(g - 1) + 1))
                        aT_high(q0 + (g + 1))
                with sc.If(r < rounds - 1):
                    hi_e(ROUND_UNITS)
                he_hi(r + 2)
                with sc.If(r < rounds - 1):
                    hi_e(ROUND_UNITS + 1)
                sc.wait_ge(unit_used, used(ROUND_UNITS - 1))
                nc.scalar.activation(ye[:, 0:HALF], bank[4][:, :], ACT.Copy).then_inc(ye_act, 1)
                with sc.If(r < rounds - 1):
                    hi_e(ROUND_UNITS + 2)
            for tb in range(TB):
                post_squares(7, tb, in_y, (acc_done, rounds * 4 + 2 * tb), in_bank)

        @block.vector
        def _(ve):
            steps = [0]

            def link(ins):
                steps[0] += 1
                ins.then_inc(dve, 1)
                ve.wait_ge(dve, steps[0])

            def split_lo(slot, source, ready):
                ve.wait_ge(hi_ready, ready)
                nc.vector.tensor_tensor(w_lo[:, slot, :], raw_slot(source), w_hi[:, slot, :].bitcast(f32),
                                        ALU.subtract).then_inc(lo_ready, 1)

            def lo(u):
                split_lo(u % SPLIT_SLOTS, slot_of(u), u + 1)

            def root(n, first, blocks=1):
                m, m4, r, t, p = (root_t[:, i, first:first + blocks] for i in range(5))
                total = sums[:, n, first:first + blocks, 0]
                ve.wait_ge(sq_done, sq_at(n, first + blocks - 1))
                if n % 2:
                    link(nc.vector.tensor_tensor(total, total, sums[:, n, first:first + blocks, 1], ALU.add))
                nc.vector.tensor_scalar(m4, total, 0.25 / D, 0.25 * EPS, ALU.mult, ALU.add)
                link(nc.vector.tensor_scalar(m, total, 1.0 / D, EPS, ALU.mult, ALU.add))
                link(nc.vector.tensor_scalar(r.bitcast(i32), m.bitcast(i32), -0.5, float(0x5F3759DF),
                                             ALU.mult, ALU.add))
                for scaled, op in ((m, "newton"), (m4, None)):
                    if blocks == 1:
                        link(nc.vector.scalar_tensor_tensor(t, r, scaled, r, ALU.mult, ALU.mult))
                    else:
                        link(nc.vector.tensor_tensor(t, r, r, ALU.mult))
                        link(nc.vector.tensor_tensor(t, t, scaled, ALU.mult))
                    if op:
                        link(nc.vector.scalar_tensor_tensor(r, t, -3.0, r, ALU.add, ALU.mult))
                link(nc.vector.tensor_scalar(p, t, -3.0 / 16, 5.0 / 8, ALU.mult, ALU.add))
                link(nc.vector.tensor_tensor(p, p, t, ALU.mult))
                link(nc.vector.scalar_tensor_tensor(rstd[:, n, first:first + blocks], p, -15.0 / 16, r,
                                                    ALU.add, ALU.mult))

            def gain_landed(n):
                if n < 2:
                    ve.wait_ge(gain_first[n], 16)
                else:
                    ve.wait_ge(gain_in[n % 2], 16 * (n // 2))

            def norm_x(n, tb):
                gain_landed(n)
                nc.vector.scalar_tensor_tensor(xn[:, tb, :], x[:, tb, :], rstd[:, n, tb:tb + 1],
                                               gain[:, n % 2, :], ALU.mult, ALU.mult).then_inc(xn_done, 1)

            def add_normed(n, tb, scaled):
                nc.vector.scalar_tensor_tensor(x[:, tb, :], scaled[:, tb, :], rstd[:, n, tb:tb + 1], x[:, tb, :],
                                               ALU.mult, ALU.add).then_inc(x_done, 1)

            def scale_bank(n, tb, to, source, ready, beside):
                gain_landed(n)
                if beside:
                    ve.wait_ge(*ready)
                else:
                    ve.wait_ge(sq_done, sq_at(n, tb))
                for half in (1, 0):
                    cols = slice(half * HALF, (half + 1) * HALF)
                    if beside and half == 0:
                        ve.wait_ge(sq_done, sq_at(n, tb) - 1)
                    nc.vector.tensor_tensor(to[:, tb, cols], source(tb, half), gain[:, n % 2, cols],
                                            ALU.mult).then_inc(yg_done, 1)
                yg[0] += 2

            def scaled_ready():
                ve.wait_ge(yg_done, yg[0])

            yg = [0]

            def input_lo(phase, blocks=range(TB)):
                for b in [2 * tb + i for tb in blocks for i in range(2)]:
                    ve.wait_ge(h_hi_done, 4 * phase + b + 1)
                    nc.vector.tensor_tensor(input_part(h_lo, phase, b), bank_blocks(phase, b),
                                            input_part(h_hi, phase, b).bitcast(f32),
                                            ALU.subtract).then_inc(h_lo_done, 1)

            nc.vector.memset(silu[:, :], 1.0).then_inc(ones_done, 1)
            root(0, 0)
            norm_x(0, 0)
            root(0, 1)
            norm_x(0, 1)
            lo(0)
            input_lo(0)
            lo(1)
            lo(2)

            def pooled(tb):
                ve.wait_ge(*((y0_psum, 1), (unit_used, 1))[tb])
                for half in range(2):
                    cols = slice(half * HALF, (half + 1) * HALF)
                    nc.vector.tensor_tensor(y[:, tb, cols], bank[4 + 2 * tb + half][:, :], scale[:, cols],
                                            ALU.mult).then_inc(y_done, 1)

            def pooled_gain(tb):
                ve.wait_ge(y_done, 2 * tb + 2)
                nc.vector.tensor_tensor(xn[:, tb, :], y[:, tb, :], gain[:, 1, :], ALU.mult).then_inc(yg_done, 1)
                yg[0] += 1

            ve.wait_ge(scale_in, 16)
            pooled(0)
            gain_landed(1)
            pooled_gain(0)
            root(1, 0)
            scaled_ready()
            add_normed(1, 0, xn)
            pooled(1)
            root(2, 0)
            norm_x(2, 0)
            pooled_gain(1)
            root(1, 1)
            input_lo(1, [0])
            scaled_ready()
            add_normed(1, 1, xn)
            root(2, 1)
            norm_x(2, 1)
            input_lo(1, [1])
            for i, (wide, at, n) in enumerate(((wf2, 0, H), (wr2, H, E))):
                ve.wait_ge(small_hi, i + 1)
                nc.vector.tensor_tensor(wide[:, :, n:2 * n], small_w[:, :, at:at + n], wide[:, :, 0:n].bitcast(f32),
                                        ALU.subtract).then_inc(small_lo, 1)

            def gated(q, used):
                ve.wait_ge(silu_done, q)
                ve.wait_ge(unit_used, used)
                ve.wait_ge(aT_psum, q - 1) if not isinstance(q, int) or q > 1 else None
                nc.vector.tensor_tensor(act[:, :], silu[:, :], bank[1][:, :], ALU.mult).then_inc(act_done, 1)

            def aT_low(q):
                ve.wait_ge(aT_hi_done, q)
                nc.vector.tensor_tensor(aT_lo[:, :], bank[2][:, :], aT_hi[:, :].bitcast(f32),
                                        ALU.subtract).then_inc(aT_lo_done, 1)

            lo(3)
            gated(1, u_up(0) + 1)
            for g in range(N_FG):
                if g < N_FG - 1:
                    lo(u_up(g + 1))
                    lo(u_down(g))
                    aT_low(g + 1)
                    lo(u_down(g) + 1)
                    gated(g + 2, u_up(g + 1) + 1)
                else:
                    lo(V_U0)
                    aT_low(g + 1)
                    lo(V_U0 + 1)
            def ffn_out(tb, half):
                return bank[4 + 2 * tb + half][:, :]

            scale_bank(3, 0, y, ffn_out, (y0_psum, 2), True)
            root(3, 0)
            scaled_ready()
            add_normed(3, 0, y)
            scale_bank(3, 1, y, ffn_out, None, False)
            root(4, 0)
            norm_x(4, 0)
            root(3, 1)
            input_lo(2, [0])
            scaled_ready()
            add_normed(3, 1, y)
            root(4, 1)
            norm_x(4, 1)
            input_lo(2, [1])
            lo(V_U0 + 2)
            lo(V_U0 + 3)
            ve.wait_ge(small_in, 48)
            ve.wait_ge(f_psum, 1)
            link(nc.vector.tensor_scalar(fz[:, :], bank[2][0:H, 0:T], bf[:, 0:1], None, ALU.add))
            nc.vector.scalar_tensor_tensor(fe[:, :], fz[:, :], -1.0, fz[:, :], ALU.mult, ALU.max).then_inc(fz_done, 1)
            link(nc.vector.tensor_scalar(fz[:, :], fz[:, :], -1.0, 0.0, ALU.mult, ALU.max))
            lo(QK_U0)
            ve.wait_ge(fl_done, 1)
            link(nc.vector.tensor_tensor(fz[:, :], fz[:, :], fl[:, :], ALU.add))
            nc.vector.tensor_tensor_scan(ncT[:, :], fz[:, :], fz[:, :], 0.0, ALU.add, ALU.bypass).then_inc(dve, 1)
            steps[0] += 1
            nc.vector.memset(ncT2[:, :].bitcast(f32), 0.0).then_inc(dve, 1)
            steps[0] += 1
            ve.wait_ge(dve, steps[0])
            link(nc.vector.tensor_copy(ncT2[0:H, :], ncT[:, :]))
            nc.vector.tensor_tensor(ncT2[LO_ROW:LO_ROW + H, :], ncT[:, :], ncT2[0:H, :].bitcast(f32),
                                    ALU.subtract).then_inc(ncT_done, 1)
            lo(QK_U0 + 1)

            def out_lo(j):
                ve.wait_ge(o_hi_done, j + 1)
                nc.vector.tensor_tensor(o_lo[:, j, :], bank[6][:, 0:T], o_hi[:, j, :].bitcast(f32),
                                        ALU.subtract).then_inc(o_lo_done, 1)

            for j in range(H // 2):
                lo(QK_U0 + j + 2)
                ve.wait_ge(q_done, j + 1)
                if j > 0:
                    ve.wait_ge(s_psum, 2 * j)
                nc.vector.tensor_copy(qk[:, T:2 * T], bank[0][:, T:2 * T]).then_inc(k_done, 1)
                if j > 0:
                    out_lo(j - 1)
                for i in range(2):
                    ve.wait_ge(s_psum, 2 * j + i + 1)
                    if j > 0:
                        ve.wait_ge(pT_psum, 2 * (j - 1) + i + 1)
                    for b in range(TB):
                        step = nc.vector.tensor_tensor_reduce(
                            out=logit[:, i, b * P:(2 * b + 1) * P], in0=bank[1 + i][:, b * P:(2 * b + 1) * P],
                            in1=consts[:, C_MASK + b * P:C_MASK + (2 * b + 1) * P], scale=1.0, scalar=NEG_INF,
                            op0=ALU.add, op1=ALU.max, accum_out=mx[:, j, 2 * i + b:2 * i + b + 1])
                    link(step)
                    nc.vector.tensor_scalar(nmx[:, j, 2 * i:2 * i + 2], mx[:, j, 2 * i:2 * i + 2], -1.0, None,
                                            ALU.mult).then_inc(mx_done, 1)
                for i in range(2):
                    ve.wait_ge(exp_done, 4 * j + 2 * i + 2)
                    link(nc.vector.reciprocal(rden[:, j, 2 * i:2 * i + 2], den[:, j, 2 * i:2 * i + 2]))
                    for b in range(TB):
                        lt = logit[:, i, b * P:(2 * b + 1) * P]
                        step = nc.vector.tensor_scalar(lt, lt, rden[:, j, 2 * i + b:2 * i + b + 1], None, ALU.mult)
                    step.then_inc(p_done, 1)
            out_lo(H // 2 - 1)
            for i in range(2):
                lo(OUT_U0 + 2 + i)
            def attn_out(tb, half):
                return bank[(1, 2, 3, 7)[2 * tb + half]][:, :]

            scale_bank(5, 0, v, attn_out, (y0_psum, 3), True)
            root(5, 0)
            scaled_ready()
            add_normed(5, 0, v)
            root(6, 0)
            norm_x(6, 0)
            scale_bank(5, 1, v, attn_out, (unit_used, MOE_U0), True)
            root(5, 1)
            scaled_ready()
            add_normed(5, 1, v)
            input_lo(3, [0])
            root(6, 1)
            norm_x(6, 1)
            input_lo(3, [1])
            for j in range(2):
                lo(MOE_U0 + j)
            iota = consts[:, C_IOTA:C_IOTA + P]
            iota8 = consts[:, C_IOTA:C_IOTA + E]
            big, more, incl, shift, base = (ctab[:, i, :] for i in range(1, 6))
            nc.vector.memset(slots_step[:, :, :], float(P))
            link(nc.vector.tensor_scalar(base, iota8, float(P), None, ALU.mult))
            ve.wait_ge(lgT_psum, 1)
            nc.vector.tensor_copy(lgT, bank[4][0:E, 0:T]).then_inc(lgT_done, 1)
            ve.wait_ge(lg_psum, 1)
            link(nc.vector.tensor_copy(lg[:, :, :], bank[5][:, 0:TB * E].rearrange("p (b e) -> p b e", e=E)))
            for tb in range(TB):
                step = nc.vector.max(top[:, tb, :], lg[:, tb, :])
            link(step)
            for tb in range(TB):
                step = nc.vector.max_index(topi[:, tb, :], top[:, tb, :], lg[:, tb, :])
            link(step)
            link(nc.vector.tensor_copy(topf[:, :, :], topi[:, :, 0:2]))
            nc.vector.tensor_tensor(gtmp[:, :, 0:1], top[:, :, 1:2], top[:, :, 0:1], ALU.subtract).then_inc(gap_done, 1)
            for tb in range(TB):
                for i in range(2):
                    step = nc.vector.tensor_scalar(m12[:, tb, i, :], iota8, topf[:, tb, i:i + 1], None, ALU.is_equal)
            link(step)
            nc.vector.tensor_tensor(mboth[:, :, :], m12[:, :, 0, :], m12[:, :, 1, :], ALU.add).then_inc(m_done, 1)
            ve.wait_ge(gexp_done, 1)
            link(nc.vector.tensor_scalar(gtmp[:, :, 2:3], gtmp[:, :, 1:2], 1.0, None, ALU.add))
            link(nc.vector.reciprocal(gate[:, :, 0:1], gtmp[:, :, 2:3]))
            link(nc.vector.tensor_tensor(gate[:, :, 1:2], gate[:, :, 0:1], gtmp[:, :, 1:2], ALU.mult))
            ve.wait_ge(rank_psum, 1)
            rank_ps = bank[5][:, 0:TB * E].rearrange("p (b e) -> p b e", e=E)
            nc.vector.tensor_scalar(over[:, :, :], rank_ps, float(P), None, ALU.is_ge)
            for tb in range(TB):
                nc.vector.tensor_tensor(rank[:, tb, :], rank_ps[:, tb, :], base, ALU.add)
            link(nc.vector.tensor_scalar(big, bank[5][:, TB * E:(TB + 1) * E], float(P), None, ALU.is_gt))
            link(nc.vector.tensor_tensor_scan(incl, big, big, 0.0, ALU.add, ALU.bypass))
            link(nc.vector.tensor_tensor(more, incl, big, ALU.subtract))
            link(nc.vector.tensor_scalar(shift, more, float(P), float(P * (E - 1)), ALU.mult, ALU.add))
            link(nc.vector.tensor_tensor(shift, shift, base, ALU.subtract))
            for tb in range(TB):
                step = nc.vector.tensor_tensor(over[:, tb, :], over[:, tb, :], shift, ALU.mult)
            link(step)
            link(nc.vector.tensor_tensor(rank[:, :, :], rank[:, :, :], over[:, :, :], ALU.add))
            for i in range(2):
                step = nc.vector.tensor_tensor(prod[:, :, i, :], m12[:, :, i, :], rank[:, :, :], ALU.mult)
            link(step)
            link(nc.vector.reduce_sum(gpos[:, :, :], prod[:, :, :, :], AX.X))
            for tb in range(TB):
                step = nc.vector.tensor_scalar(sel2[:, tb, :], iota, gpos[:, tb, 0:1], None, ALU.is_equal)
            link(step)
            for tb in range(TB):
                nc.vector.scalar_tensor_tensor(sel[:, tb, :], iota, gpos[:, tb, 1:2], sel2[:, tb, :], ALU.is_equal,
                                               ALU.add).then_inc(sel_ready, 1)
            for tb in range(TB):
                step = nc.vector.tensor_scalar(gsel[:, tb, :], iota, gpos[:, tb, 0:1], gate[:, tb, 0:1],
                                               ALU.is_equal, ALU.mult)
            ve.wait_ge(sel_ready, 2)
            for tb in range(TB):
                step = nc.vector.tensor_scalar(sel2[:, tb, :], iota, gpos[:, tb, 1:2], gate[:, tb, 1:2],
                                               ALU.is_equal, ALU.mult)
            link(step)
            link(nc.vector.tensor_tensor(gsel[:, :, :], gsel[:, :, :], sel2[:, :, :], ALU.add))
            nc.vector.tensor_scalar(gpos[:, :, :], gpos[:, :, :], float(-P), None, ALU.add).then_inc(sel_done, 1)
            link(nc.vector.tensor_scalar(rtab[:, 0:1], ctab[0:1, 3, E - 1:E], float(E), None, ALU.add))
            for i in range(X_ROUNDS):
                link(nc.vector.tensor_scalar(ctab[0:1, 6, :], ctab[0:1, 3, :], float(i), None, ALU.is_le))
                link(nc.vector.reduce_sum(rtab[:, 1 + i:2 + i], ctab[0:1, 6, :], AX.X))
            link(nc.vector.tensor_scalar(rtab[:, 1:4], rtab[:, 1:4], float(E - 1), None, ALU.min))
            nc.vector.tensor_copy(rtab_i[:, :], rtab[:, :]).then_inc(rtab_done, 1)


            def he_lo(r1):
                for i in range(2):
                    ve.wait_ge(he_hi_done, r1 * 2 - (1 - i))
                    nc.vector.tensor_tensor(h_lo[:, 4 * i:4 * i + 4, 0:P], bank_blocks(3, 6 + i),
                                            h_hi[:, 4 * i:4 * i + 4, 0:P].bitcast(f32),
                                            ALU.subtract).then_inc(he_lo_done, 1)

            lo(MOE_U0 + 2)
            he_lo(1)
            ve.wait_ge(rtab_done, 1)
            rounds = ve.value_load(rtab_i[0:1, 0:1], min_val=E, max_val=E + X_ROUNDS)
            with ve.Fori(0, rounds) as r:
                def lo_e(j):
                    split_lo((MOE_U0 + j) % SPLIT_SLOTS, moe_slot(j), r * ROUND_UNITS + (MOE_U0 + j + 1))

                def used(j):
                    return r * ROUND_UNITS + (MOE_U0 + j + 1)

                q0 = r * N_EG + N_FG
                for j in range(3, 6):
                    lo_e(j)
                gated(q0 + 1, used(j_up(0) + 1))
                for g in range(N_EG):
                    if g < N_EG - 1:
                        if g > 0:
                            lo_e(j_gate(g + 1))
                            lo_e(j_gate(g + 1) + 1)
                        lo_e(j_up(g + 1))
                        lo_e(j_up(g + 1) + 1)
                        aT_low(q0 + (g + 1))
                        lo_e(j_down(g))
                        lo_e(j_down(g) + 1)
                        gated(q0 + (g + 2), used(j_up(g + 1) + 1))
                    else:
                        lo_e(j_down(g))
                        lo_e(j_down(g) + 1)
                        aT_low(q0 + (g + 1))
                with ve.If(r < rounds - 1):
                    lo_e(ROUND_UNITS)
                he_lo(r + 2)
                with ve.If(r < rounds - 1):
                    lo_e(ROUND_UNITS + 1)
                ve.wait_ge(unit_used, used(ROUND_UNITS - 1))
                nc.vector.tensor_copy(ye[:, HALF:D], bank[5][:, :]).then_inc(ye_dve, 1)
                with ve.If(r < rounds - 1):
                    lo_e(ROUND_UNITS + 2)
                ve.wait_ge(acc_done, r * 4 + 2)
                for tb in range(TB):
                    ve.wait_ge(sc_psum, r * 2 + (tb + 1))
                    for half in range(2):
                        cols = slice(half * HALF, (half + 1) * HALF)
                        nc.vector.tensor_tensor(y[:, tb, cols], y[:, tb, cols], bank[4 + 2 * tb + half][:, :],
                                                ALU.add).then_inc(acc_done, 1)
            ve.wait_ge(acc_done, rounds * 4 + 2)
            gain_landed(7)
            nc.vector.tensor_tensor(xn[:, 1, :], y[:, 1, :], gain[:, 1, :], ALU.mult).then_inc(yg_done, 1)
            yg[0] += 1
            root(7, 0, TB)
            scaled_ready()
            ve.wait_ge(pool_scaled, 1)
            for tb in range(TB):
                for half in range(2):
                    cols = slice(half * HALF, (half + 1) * HALF)
                    nc.vector.scalar_tensor_tensor(x[:, tb, cols], xn[:, tb, cols], rstd[:, 7, tb:tb + 1],
                                                   x[:, tb, cols], ALU.mult, ALU.add).then_inc(x_done, 1)

        @block.tensor
        def _(pe):
            mm = nc.tensor.matmul

            def three(out, a_hi, a_lo, b_hi, b_lo, first, last):
                mm(out, a_hi, b_hi, start=first, stop=False)
                mm(out, a_hi, b_lo, start=False, stop=False)
                return mm(out, a_lo, b_hi, start=False, stop=last)

            def keep_warm(n, source=ident, to=bank[0]):
                for _ in range(n):
                    mm(to[:, 0:P], source, source, start=True, stop=True)

            def weights(u, n):
                s = u % SPLIT_SLOTS
                pe.wait_ge(lo_ready, u + 1)
                return part(w_hi, s, n), part(w_lo, s, n)

            def input_transposed(phase, tb):
                pe.wait_ge(xn_done, 2 * phase + tb + 1)
                for i in range(2):
                    for k in range(4):
                        c = (4 * i + k) * P
                        step = nc.tensor.transpose(bank[2 * tb + i][:, k * P:(k + 1) * P], xn[:, tb, c:c + P],
                                                   ident)
                    step.then_inc(tr_done, 1)

            def three_t(to, wide, n):
                for k in range(KB):
                    step = three(to, wide[:, k, 0:n], wide[:, k, n:2 * n], h_hi[:, k, :], h_lo[:, k, :],
                                 k == 0, k == KB - 1)
                return step

            pe.wait_ge(ones_done, 1)
            keep_warm(WARM_START, silu[:, 0:P])
            pe.wait_ge(bands_in, 16)
            pe.wait_ge(xn_done, 1)

            def pool_first(k):
                mm(bank[k // 2][:, (k % 2) * T:(k % 2 + 1) * T], xn[:, 0, k * P:(k + 1) * P], bands[:, k // 2, 0:T],
                   start=True, stop=False)

            def pool_second(k):
                return mm(bank[k // 2][:, (k % 2) * T + P:(k % 2 + 1) * T], xn[:, 1, k * P:(k + 1) * P],
                          bands[:, k // 2, T:T + P], start=False, stop=True)

            for k in range(0, KB, 2):
                pool_first(k)
            pe.wait_ge(xn_done, 2)
            for k in range(0, KB, 2):
                pool_second(k)
                pool_first(k + 1)
                pool_second(k + 1).then_inc(tr_done, 1)
            hi, lo = weights(0, FG)
            for tb in range(TB):
                tok = slice(tb * P, (tb + 1) * P)
                for g in range(POOL_G):
                    if tb == 0:
                        pe.wait_ge(h_lo_done, g + 1)
                    to = bank[4 + 2 * tb + g // 2][:, (g % 2) * FG:(g % 2 + 1) * FG]
                    for i in range(2):
                        k = 2 * g + i
                        step = three(to, h_hi[:, k, tok], h_lo[:, k, tok], hi[:, k, :], lo[:, k, :], i == 0, i == 1)
                step.then_inc((y0_psum, unit_used)[tb], 1)

            pe.wait_ge(consts_in, 16)
            keep_warm(WARM[0])

            def ffn_in(u, to, blocks=range(TB)):
                hi, lo = weights(u, FG)
                for tb in blocks:
                    tok = slice(tb * P, (tb + 1) * P)
                    for k in range(KB):
                        step = three(to[:, tb * FG:(tb + 1) * FG], h_hi[:, k, tok], h_lo[:, k, tok],
                                     hi[:, k, :], lo[:, k, :], k == 0, k == KB - 1)
                if TB - 1 in blocks:
                    step.then_inc(unit_used, 1)

            def transpose_act(q, sources):
                pe.wait_ge(act_done, q)
                pe.wait_ge(aT_lo_done, q - 1) if not isinstance(q, int) or q > 1 else None
                for i, source in enumerate(sources):
                    step = nc.tensor.transpose(bank[2][:, i * P:(i + 1) * P], source, ident)
                step.then_inc(aT_psum, 1)

            for tb in range(TB):
                input_transposed(1, tb)
                pe.wait_ge(h_lo_done, 4 + 2 * tb + 2)
                ffn_in(u_gate(0), bank[0], [tb])
                ffn_in(u_up(0), bank[1], [tb])
            pe.wait_ge(x_done, 2)
            for g in range(N_FG):
                if g < N_FG - 1:
                    pe.wait_ge(silu_done, g + 1)
                    ffn_in(u_gate(g + 1), bank[0])
                transpose_act(g + 1, [act[:, tb * FG + f * P:tb * FG + (f + 1) * P] for f in range(2) for tb in range(TB)])
                if g < N_FG - 1:
                    ffn_in(u_up(g + 1), bank[1])
                pe.wait_ge(aT_lo_done, g + 1)
                hi, lo = weights(u_down(g), D)
                for tb in range(TB):
                    for half in range(2):
                        cols = slice(half * HALF, (half + 1) * HALF)
                        for f in range(2):
                            tok = slice(f * T + tb * P, f * T + (tb + 1) * P)
                            step = three(bank[4 + 2 * tb + half][:, :], aT_hi[:, tok], aT_lo[:, tok],
                                         hi[:, f, cols], lo[:, f, cols], g == 0 and f == 0, g == N_FG - 1 and f == 1)
                    if g == N_FG - 1 and tb == 0:
                        step.then_inc(y0_psum, 1)
                step.then_inc(unit_used, 1)

            def v_unit(i, blocks=range(TB)):
                hi, lo = weights(V_U0 + i, HALF)
                for tb in blocks:
                    tok = slice(tb * P, (tb + 1) * P)
                    for k in range(4):
                        kb = 4 * (i % 2) + k
                        step = three(bank[4 + 2 * (i // 2) + tb][:, :], h_hi[:, kb, tok], h_lo[:, kb, tok],
                                     hi[:, k, :], lo[:, k, :], kb == 0, kb == KB - 1)
                if TB - 1 in blocks:
                    step.then_inc(unit_used, 1)

            keep_warm(WARM[1])
            for tb in range(TB):
                input_transposed(2, tb)
                pe.wait_ge(h_lo_done, 2 * 4 + 2 * tb + 2)
                v_unit(0, [tb])
                v_unit(1, [tb])
            pe.wait_ge(small_lo, 2)
            three_t(bank[2][0:H, 0:T], wf2, H).then_inc(f_psum, 1)
            v_unit(2)
            v_unit(3)

            def head_outputs(j):
                for i in range(2):
                    pe.wait_ge(p_done, 2 * j + i + 1)
                    if j > 0:
                        pe.wait_ge(pT_done, 2 * (j - 1) + i + 1)
                    nc.tensor.transpose(bank[4 + i][:, 0:P], logit[:, i, 0:P], ident)
                    nc.tensor.transpose(bank[4 + i][:, P:2 * P], logit[:, i, P:2 * P], ident)
                    nc.tensor.transpose(bank[4 + i][:, 2 * P:3 * P], logit[:, i, 2 * P:3 * P], ident).then_inc(pT_psum, 1)
                if j > 0:
                    pe.wait_ge(o_lo_done, j)
                for i in range(2):
                    pe.wait_ge(pT_done, 2 * j + i + 1)
                    c = (2 * j + i) * HD
                    to = bank[6][i * HD:(i + 1) * HD, :]
                    mm(to[:, 0:T], v[:, 0, c:c + HD], pT[:, i, 0:T], start=True, stop=False)
                    step = mm(to[:, P:T], v[:, 1, c:c + HD], pT[:, i, T:3 * P], start=False, stop=True)
                step.then_inc(o_psum, 1)

            for j in range(H // 2):
                hi, lo = weights(QK_U0 + j, T)
                if j == 0:
                    pe.wait_ge(v_done, 4)
                    pe.wait_ge(heads_in, 16)
                    pe.wait_ge(ncT_done, 1)
                for i in range(2):
                    for k in range(KB):
                        cols = slice(i * P, (i + 1) * P)
                        step = three(bank[0][:, i * T:(i + 1) * T], hi[:, k, cols], lo[:, k, cols],
                                     h_hi[:, k, :], h_lo[:, k, :], k == 0, k == KB - 1)
                step.then_inc(unit_used, 1)
                if j > 0:
                    head_outputs(j - 1)
                pe.wait_ge(q_done, j + 1)
                pe.wait_ge(k_done, j + 1)
                for i in range(2):
                    if j > 0:
                        pe.wait_ge(mx_done, 2 * (j - 1) + i + 1)
                    h0 = i * HD
                    for b in range(TB):
                        to = bank[1 + i][:, b * P:b * P + (b + 1) * P]
                        mm(to, qk[h0:h0 + HD, b * P:(b + 1) * P], qk[h0:h0 + HD, T:T + (b + 1) * P],
                           start=True, stop=False)
                        step = mm(to, head_row[:, 2 * j + i, :], ncT2[:, 0:(b + 1) * P], start=False, stop=True)
                    step.then_inc(s_psum, 1)
            head_outputs(H // 2 - 1)
            pe.wait_ge(o_lo_done, H // 2)
            pe.wait_ge(mx_done, H)
            for w, tb in ((0, 0), (0, 1), (1, 0), (2, 0), (3, 0), (1, 1), (2, 1), (3, 1)):
                hi, lo = weights(OUT_U0 + w, D)
                tok = slice(tb * P, (tb + 1) * P)
                for half in range(2):
                    cols = slice(half * HALF, (half + 1) * HALF)
                    for i in range(2):
                        k = 2 * w + i
                        step = three(bank[(1, 2, 3, 7)[2 * tb + half]][:, :], o_hi[:, k, tok], o_lo[:, k, tok],
                                     hi[:, i, cols], lo[:, i, cols], k == 0, k == KB - 1)
                if w == 3 and tb == 0:
                    step.then_inc(y0_psum, 1)
                if tb == 1:
                    step.then_inc(unit_used, 1)

            keep_warm(WARM[2])
            input_transposed(3, 0)
            keep_warm(WARM[4], to=bank[5])
            input_transposed(3, 1)
            pe.wait_ge(h_lo_done, 4 * 4)
            three_t(bank[4][0:E, 0:T], wr2, E).then_inc(lgT_psum, 1)
            pe.wait_ge(lgT_done, 1)
            for tb in range(TB):
                step = nc.tensor.transpose(bank[5][:, tb * E:(tb + 1) * E], lgT[:, tb * P:(tb + 1) * P], ident[0:E, 0:E])
            step.then_inc(lg_psum, 1)
            keep_warm(WARM[5])
            pe.wait_ge(m_done, 1)
            ones, before = consts[:, C_ONES:C_ONES + P], consts[:, C_TRIS:C_TRIS + P]
            mm(bank[5][:, 0:E], before, mboth[:, 0, :], start=True, stop=True)
            mm(bank[5][:, E:2 * E], ones, mboth[:, 0, :], start=True, stop=False)
            mm(bank[5][:, E:2 * E], before, mboth[:, 1, :], start=False, stop=True)
            mm(bank[5][:, 2 * E:3 * E], ones, mboth[:, 0, :], start=True, stop=False)
            mm(bank[5][:, 2 * E:3 * E], ones, mboth[:, 1, :], start=False, stop=True).then_inc(rank_psum, 1)

            def gather(r1):
                pe.wait_ge(sel_ready, r1 + 1)
                for k in range(KB):
                    for tb in range(TB):
                        step = mm(bank[6 + k // 4][:, (k % 4) * P:(k % 4 + 1) * P], xn[:, tb, k * P:(k + 1) * P],
                                  sel[:, tb, :], start=(tb == 0), stop=(tb == 1))
                    if k % 4 == 3:
                        step.then_inc(he_psum, 1)

            keep_warm(WARM[3])
            gather(1)
            pe.wait_ge(rtab_done, 1)
            rounds = pe.value_load(rtab_i[0:1, 0:1], min_val=E, max_val=E + X_ROUNDS)
            def weights_e(r, j, n):
                s = (MOE_U0 + j) % SPLIT_SLOTS
                pe.wait_ge(lo_ready, r * ROUND_UNITS + (MOE_U0 + j + 1))
                return part(w_hi, s, n), part(w_lo, s, n)

            def expert_in(r, j, to, tokens=None):
                for i in range(2):
                    if tokens is not None:
                        pe.wait_ge(he_lo_done, tokens + i)
                    hi, lo = weights_e(r, j + i, HALF)
                    for k in range(4):
                        kb = 4 * i + k
                        step = three(to[:, :], h_hi[:, kb, 0:P], h_lo[:, kb, 0:P], hi[:, k, :], lo[:, k, :],
                                     kb == 0, kb == KB - 1)
                    step.then_inc(unit_used, 1)

            pe.wait_ge(silu_done, N_FG)
            expert_in(0, j_gate(0), bank[0], 1)
            with pe.Fori(0, rounds) as r:
                q0 = r * N_EG + N_FG
                pe.wait_ge(act_done, q0)
                expert_in(r, j_up(0), bank[1])
                pe.wait_ge(sel_done, r + 1)
                for tb in range(TB):
                    step = nc.tensor.transpose(bank[3][:, tb * P:(tb + 1) * P], gsel[:, tb, :], ident)
                step.then_inc(gT_psum, 1)
                for g in range(N_EG):
                    if g < N_EG - 1:
                        pe.wait_ge(silu_done, q0 + (g + 1))
                        expert_in(r, j_gate(g + 1), bank[0])
                    transpose_act(q0 + (g + 1), [act[:, f * P:(f + 1) * P] for f in range(4)])
                    if g < N_EG - 1:
                        expert_in(r, j_up(g + 1), bank[1])
                    else:
                        pe.wait_ge(acc_done, r * 4 + 2)
                        gather(r + 2)
                    pe.wait_ge(aT_lo_done, q0 + (g + 1))
                    if g == 0:
                        pe.wait_ge(acc_done, r * 4 + 2)
                    for i in range(2):
                        hi, lo = weights_e(r, j_down(g) + i, D)
                        for half in range(2):
                            cols = slice(half * HALF, (half + 1) * HALF)
                            for f in range(2):
                                blk = slice((2 * i + f) * P, (2 * i + f + 1) * P)
                                step = three(bank[4 + half][:, :], aT_hi[:, blk], aT_lo[:, blk], hi[:, f, cols],
                                             lo[:, f, cols], g == 0 and i == 0 and f == 0,
                                             g == N_EG - 1 and i == 1 and f == 1)
                        step.then_inc(unit_used, 1)
                with pe.If(r < rounds - 1):
                    pe.wait_ge(silu_done, q0 + N_EG)
                    expert_in(r, ROUND_UNITS + j_gate(0), bank[0], r * 2 + 3)
                pe.wait_ge(ye_act, r + 1)
                pe.wait_ge(ye_dve, r + 1)
                pe.wait_ge(gT_done, r + 1)
                for tb in range(TB):
                    if tb == 1:
                        pe.wait_ge(he_lo_done, r * 2 + 4)
                    for half in range(2):
                        step = mm(bank[4 + 2 * tb + half][:, :], gselT[:, tb * P:(tb + 1) * P],
                                  ye[:, half * HALF:(half + 1) * HALF], start=True, stop=True)
                    step.then_inc(sc_psum, 1)

        @block.gpsimd
        def _(po):
            free = {2: (xn_done, 2), 3: (x_done, 2), 4: (xn_done, 4), 5: (x_done, 4), 6: (xn_done, 6), 7: (x_done, 6)}
            for n in range(2, 8):
                po.wait_ge(*free[n])
                po.dma_start(gain[:, n % 2, :],
                             norm_g[n // 4, n % 4:n % 4 + 1, :].to_broadcast([P, D])).then_inc(gain_in[n % 2], 16)
                if n == 2:
                    po.wait_ge(y_done, 4)
                    po.dma_start(head_row[:, :, :], heads_d.bitcast(f32r)).then_inc(heads_in, 16)
            po.wait_ge(unit_used, MOE_U0)
            for tb in range(TB):
                nc.gpsimd.memset(y[:, tb, :], 0.0).then_inc(acc_done, 1)
            po.wait_ge(rtab_done, 1)
            rounds = po.value_load(rtab_i[0:1, 0:1], min_val=E, max_val=E + X_ROUNDS)
            with po.Fori(0, rounds) as r:
                po.wait_ge(gT_psum, r + 1)
                po.wait_ge(sel_done, r + 1)
                assert select(po, nc.gpsimd, pool_step, r * SELECT_STEPS, gpos, gpos_next, slots_step, gate, sel, sel2,
                              gsel, consts, sel_ready, r + 3, sel_done, ALU) == SELECT_STEPS
            po.wait_ge(gain_in[1], 16 * 3)
            po.wait_ge(acc_done, rounds * 4 + 2)
            nc.gpsimd.tensor_tensor(xn[:, 0, :], y[:, 0, :], gain[:, 1, :], ALU.mult).then_inc(pool_scaled, 1)


_INS = ["x", "norm_g", "pool_w", "pool_scale", "attn_w_in", "attn_b_f", "attn_w_out", "ffn_w_gate", "ffn_w_up",
        "ffn_w_down", "moe_w_router", "moe_w_gate", "moe_w_up", "moe_w_down"]


def _constants():
    s, t = np.arange(P)[:, None], np.arange(P)[None, :]
    c = np.zeros((P, C_ALL), np.float32)
    c[:, C_IDENT:C_IDENT + P] = s == t
    c[:, C_ONES:C_ONES + P] = 1
    c[:, C_TRIS:C_TRIS + P] = s < t
    causal = np.where(t <= s, 0, NEG_INF)
    c[:, C_MASK:C_MASK + P] = causal
    c[:, C_MASK + 2 * P:C_MASK + 3 * P] = causal
    c[:, C_IOTA:C_IOTA + P] = t
    tok = np.arange(T)
    bands = np.zeros((P, POOL_G, 3 * P), np.float32)
    for g, w in enumerate(POOL_WINDOWS):
        full = ((tok[:, None] <= tok[None, :]) & (tok[:, None] > tok[None, :] - w)) / np.minimum(tok + 1, w)[None, :]
        full = full - np.eye(T)
        bands[:, g, 0:T] = full[0:P]
        bands[:, g, T:] = full[P:, P:]
    heads = np.zeros((LO_ROW + H, H, P), np.float32)
    for h in range(H):
        heads[h, h, :] = heads[LO_ROW + h, h, :] = 1
    return {"consts": c, "bands": bands, "heads": heads}


def kernel(**inputs):
    import concourse.bacc as bacc
    from concourse.bass_utils import run_bass_kernel_spmd

    nc = bacc.Bacc("TRN2", target_bir_lowering=False, num_devices=1)
    arrays, args = {}, []
    for name, a in [(n, np.ascontiguousarray(inputs[n])) for n in _INS] + list(_constants().items()):
        arrays[f"in_{name}"] = a
        args.append(nc.dram_tensor(f"in_{name}", a.shape, mybir.dt.from_np(a.dtype), kind="ExternalInput").ap())
    args.append(nc.dram_tensor("out_x", (1, T, D), mybir.dt.float32, kind="ExternalOutput").ap())
    trunk(nc, *args)
    result = run_bass_kernel_spmd(nc, [arrays], core_ids=[0])
    return result.results[0]["out_x"]
```
